# Optimizing a Trainium2 kernel written in Bass

```python
import jax, jax.numpy as jnp
from jax import lax
import numpy as np

D_MODEL = 1024
BATCH = 1
SEQ = 512
DEPTH = 1

HEAD_DIM = 64
NORM_EPS = 1e-6
RWKV_HEADS = 8
RWKV_WIDTH = RWKV_HEADS * HEAD_DIM
LORA_DECAY = 64
LORA_AAA = 64
LORA_GATE = 128
RWKV_COLS = 3 * RWKV_WIDTH + LORA_DECAY + LORA_AAA + LORA_GATE
RWKV_SPLITS = (RWKV_WIDTH, 2 * RWKV_WIDTH, 3 * RWKV_WIDTH,
               3 * RWKV_WIDTH + LORA_DECAY, 3 * RWKV_WIDTH + LORA_DECAY + LORA_AAA)
RWKV_GN_EPS = 64e-5
CONV_WIDTH = 512
CONV_K = 3
CONV_COLS = 3 * CONV_WIDTH
ATTN_GROUPS = ((128, 1), (512, 4), (2048, 16))
HEADS_PER_GROUP = 4
ATTN_HEADS = HEADS_PER_GROUP * len(ATTN_GROUPS)
ATTN_WIDTH = ATTN_HEADS * HEAD_DIM
ATTN_COLS = 3 * ATTN_WIDTH
ATTN_OUT_WIDTH = HEADS_PER_GROUP * HEAD_DIM
ALIBI_MAX_EXP = 8.0
N_BRANCH = 3
GATE_COLS = N_BRANCH * D_MODEL
IN_COLS = RWKV_COLS + CONV_COLS + ATTN_COLS + GATE_COLS
IN_SPLITS = (RWKV_COLS, RWKV_COLS + CONV_COLS, RWKV_COLS + CONV_COLS + ATTN_COLS)
BRANCH_ROWS = RWKV_WIDTH + CONV_WIDTH + ATTN_OUT_WIDTH
D_FF = ((8 * D_MODEL + 767) // 768) * 256

kernel_name = "hybrid_rwkv7_shortconv_dilatedattn_gated"

def rmsnorm(x, g):
    xf = x.astype(jnp.float32)
    y = xf * lax.rsqrt(jnp.mean(xf * xf, axis=-1, keepdims=True) + NORM_EPS)
    return (y * g.astype(jnp.float32)).astype(x.dtype)

def token_shift(t):
    return jnp.pad(t, ((0, 0), (1, 0), (0, 0)))[:, :-1]

def rwkv7_step(state, inp):
    r, w, k, v, a, b = inp
    sa = jnp.einsum('bhvk,bhk->bhv', state, a)
    state = state * w[:, :, None, :] + sa[..., None] * b[:, :, None, :] + v[..., None] * k[:, :, None, :]
    y = jnp.einsum('bhvk,bhk->bhv', state, r)
    return state, y

def rwkv7_time_mix(p, mu, w0, w_up, a0, a_up, g_up, k_k, k_a, r_k, ln_w, ln_b):
    bsz, seq, _ = p.shape
    xm = p + (token_shift(p) - p) * mu
    r, k, v, wl, al, gl = jnp.split(xm, RWKV_SPLITS, axis=-1)
    w_log = -jax.nn.softplus(-(w0 + jnp.tanh(wl) @ w_up)) - 0.5
    a = jax.nn.sigmoid(a0 + al @ a_up)
    g = jax.nn.sigmoid(gl) @ g_up

    def heads(t):
        return t.astype(jnp.float32).reshape(bsz, seq, RWKV_HEADS, HEAD_DIM)

    kk = heads(k * k_k)
    kk = kk * lax.rsqrt(jnp.maximum(jnp.sum(kk * kk, axis=-1, keepdims=True), 1e-12))
    k = k * (1 + (a - 1) * k_a)
    rh, kh, vh, ah = heads(r), heads(k), heads(v), heads(a)
    decay = jnp.exp(-jnp.exp(heads(w_log)))
    xs = tuple(jnp.moveaxis(t, 1, 0) for t in (rh, decay, kh, vh, -kk, kk * ah))
    state0 = jnp.zeros((bsz, RWKV_HEADS, HEAD_DIM, HEAD_DIM), jnp.float32)
    _, y = lax.scan(rwkv7_step, state0, xs)
    y = jnp.moveaxis(y, 0, 1)
    mean = jnp.mean(y, axis=-1, keepdims=True)
    var = jnp.mean(jnp.square(y - mean), axis=-1, keepdims=True)
    y = (y - mean) * lax.rsqrt(var + RWKV_GN_EPS)
    y = y * ln_w.astype(jnp.float32).reshape(RWKV_HEADS, HEAD_DIM) + ln_b.astype(jnp.float32).reshape(RWKV_HEADS, HEAD_DIM)
    y = y + jnp.sum(rh * kh * r_k.astype(jnp.float32), axis=-1, keepdims=True) * vh
    return (y.reshape(bsz, seq, RWKV_WIDTH) * g.astype(jnp.float32)).astype(p.dtype)

def short_conv_mix(p, conv_w):
    seq = p.shape[1]
    b_gate, c_gate, xc = jnp.split(p, 3, axis=-1)
    u = jnp.pad(c_gate * xc, ((0, 0), (CONV_K - 1, 0), (0, 0)))
    y = conv_w[0] * u[:, 0:seq] + conv_w[1] * u[:, 1:seq + 1] + conv_w[2] * u[:, 2:seq + 2]
    return b_gate * y

def alibi_slopes():
    return jnp.exp2(-ALIBI_MAX_EXP * jnp.arange(1, ATTN_HEADS + 1, dtype=jnp.float32) / ATTN_HEADS)

def dilated_window_group(q, k, v, slopes, window, dilation):
    bsz, seq, hg, e = q.shape
    blk = window // dilation
    sub_len = seq // dilation
    n_blk = -(-sub_len // blk)
    pad = n_blk * blk - sub_len

    def to_blocks(t):
        t = t.reshape(bsz, sub_len, dilation, hg, e).transpose(0, 2, 1, 3, 4)
        t = jnp.pad(t, ((0, 0), (0, 0), (0, pad), (0, 0), (0, 0)))
        return t.reshape(bsz, dilation, n_blk, blk, hg, e)

    def with_prev(t):
        prev = jnp.pad(t, ((0, 0), (0, 0), (1, 0), (0, 0), (0, 0), (0, 0)))[:, :, :-1]
        return jnp.concatenate([prev, t], axis=3)

    qb = to_blocks(q)
    kc = with_prev(to_blocks(k))
    vc = with_prev(to_blocks(v))
    s = jnp.einsum('bdnqhe,bdnkhe->bdnhqk', qb, kc) * (HEAD_DIM ** -0.5)
    steps = blk + jnp.arange(blk)[:, None] - jnp.arange(2 * blk)[None, :]
    in_window = (steps >= 0) & (steps <= blk)
    exists = (jnp.arange(n_blk)[:, None] > 0) | (jnp.arange(2 * blk)[None, :] >= blk)
    mask = in_window[None] & exists[:, None, :]
    alibi = -slopes[:, None, None] * (steps * dilation).astype(jnp.float32)[None]
    s = jnp.where(mask[None, None, :, None], s + alibi[None, None, None], -jnp.inf)
    m = jnp.max(s, axis=-1, keepdims=True)
    pexp = jnp.exp(s - m)
    l = jnp.sum(pexp, axis=-1, keepdims=True)
    o = jnp.einsum('bdnhqk,bdnkhe->bdnqhe', pexp / l, vc)
    lse = jnp.transpose((m + jnp.log(l))[..., 0], (0, 1, 2, 4, 3))

    def from_blocks(t):
        t = t.reshape((bsz, dilation, n_blk * blk) + t.shape[4:])[:, :, :sub_len]
        t = jnp.moveaxis(t, 1, 2)
        return t.reshape((bsz, seq) + t.shape[3:])

    return from_blocks(o), from_blocks(lse)

def dilated_attention_mix(p):
    bsz, seq, _ = p.shape
    q, k, v = (t.astype(jnp.float32).reshape(bsz, seq, ATTN_HEADS, HEAD_DIM) for t in jnp.split(p, 3, axis=-1))
    slopes = alibi_slopes()
    outs, lses = [], []
    for gi, (window, dilation) in enumerate(ATTN_GROUPS):
        sl = slice(gi * HEADS_PER_GROUP, (gi + 1) * HEADS_PER_GROUP)
        o, lse = dilated_window_group(q[:, :, sl], k[:, :, sl], v[:, :, sl], slopes[sl], window, dilation)
        outs.append(o)
        lses.append(lse)
    o = jnp.stack(outs)
    wts = jax.nn.softmax(jnp.stack(lses), axis=0)
    y = jnp.sum(wts[..., None] * o, axis=0)
    return y.reshape(bsz, seq, ATTN_OUT_WIDTH).astype(p.dtype)

def setup_inputs(seed: int = 0) -> dict:
    key = jax.random.key(seed)
    ks = jax.random.split(key, 32)
    f32 = jnp.float32

    def nrm(k, shape, scale):
        return jax.random.normal(k, shape, f32) * scale

    def gain(k, shape):
        return 1.0 + 0.05 * jax.random.normal(k, shape, f32)

    w_branch = jnp.concatenate([
        nrm(ks[20], (DEPTH, RWKV_WIDTH, D_MODEL), RWKV_WIDTH ** -0.5),
        nrm(ks[21], (DEPTH, CONV_WIDTH, D_MODEL), CONV_WIDTH ** -0.5),
        nrm(ks[22], (DEPTH, ATTN_OUT_WIDTH, D_MODEL), ATTN_OUT_WIDTH ** -0.5)], axis=1)
    return {
        "x": nrm(ks[0], (BATCH, SEQ, D_MODEL), 1.0),
        "norm_mix_pre": gain(ks[1], (DEPTH, D_MODEL)),
        "norm_mix_post": gain(ks[2], (DEPTH, D_MODEL)),
        "norm_ffn_pre": gain(ks[3], (DEPTH, D_MODEL)),
        "norm_ffn_post": gain(ks[4], (DEPTH, D_MODEL)),
        "w_in": nrm(ks[5], (DEPTH, D_MODEL, IN_COLS), D_MODEL ** -0.5),
        "rwkv_mu": jax.random.uniform(ks[6], (DEPTH, RWKV_COLS), f32),
        "rwkv_w0": jax.random.uniform(ks[7], (DEPTH, RWKV_WIDTH), f32, -6.0, 1.0),
        "rwkv_w_up": nrm(ks[8], (DEPTH, LORA_DECAY, RWKV_WIDTH), 0.5 * LORA_DECAY ** -0.5),
        "rwkv_a0": nrm(ks[9], (DEPTH, RWKV_WIDTH), 0.5),
        "rwkv_a_up": nrm(ks[10], (DEPTH, LORA_AAA, RWKV_WIDTH), 0.5 * LORA_AAA ** -0.5),
        "rwkv_g_up": nrm(ks[11], (DEPTH, LORA_GATE, RWKV_WIDTH), LORA_GATE ** -0.5),
        "rwkv_k_k": 0.85 + 0.05 * jax.random.normal(ks[12], (DEPTH, RWKV_WIDTH), f32),
        "rwkv_k_a": gain(ks[13], (DEPTH, RWKV_WIDTH)),
        "rwkv_r_k": nrm(ks[14], (DEPTH, RWKV_HEADS, HEAD_DIM), 0.1),
        "rwkv_ln_w": gain(ks[15], (DEPTH, RWKV_WIDTH)),
        "rwkv_ln_b": nrm(ks[16], (DEPTH, RWKV_WIDTH), 0.02),
        "conv_w": nrm(ks[17], (DEPTH, CONV_K, CONV_WIDTH), CONV_K ** -0.5),
        "w_branch": w_branch,
        "w_out": nrm(ks[23], (DEPTH, D_MODEL, D_MODEL), D_MODEL ** -0.5),
        "w_ffn_in": nrm(ks[24], (DEPTH, D_MODEL, 2 * D_FF), D_MODEL ** -0.5),
        "w_ffn_out": nrm(ks[25], (DEPTH, D_FF, D_MODEL), D_FF ** -0.5),
    }

def reference(x, norm_mix_pre, norm_mix_post, norm_ffn_pre, norm_ffn_post, w_in, rwkv_mu, rwkv_w0,
              rwkv_w_up, rwkv_a0, rwkv_a_up, rwkv_g_up, rwkv_k_k, rwkv_k_a, rwkv_r_k, rwkv_ln_w, rwkv_ln_b,
              conv_w, w_branch, w_out, w_ffn_in, w_ffn_out):
    for l in range(DEPTH):
        h = rmsnorm(x, norm_mix_pre[l])
        proj = h @ w_in[l]
        p_rwkv, p_conv, p_attn, p_gate = jnp.split(proj, IN_SPLITS, axis=-1)
        y_a = rwkv7_time_mix(p_rwkv, rwkv_mu[l], rwkv_w0[l], rwkv_w_up[l], rwkv_a0[l], rwkv_a_up[l],
                             rwkv_g_up[l], rwkv_k_k[l], rwkv_k_a[l], rwkv_r_k[l], rwkv_ln_w[l], rwkv_ln_b[l])
        y_b = short_conv_mix(p_conv, conv_w[l])
        y_c = dilated_attention_mix(p_attn)
        g_a, g_b, g_c = jnp.split(jax.nn.sigmoid(p_gate), N_BRANCH, axis=-1)
        wb = w_branch[l]
        merged = (g_a * (y_a @ wb[:RWKV_WIDTH])
                  + g_b * (y_b @ wb[RWKV_WIDTH:RWKV_WIDTH + CONV_WIDTH])
                  + g_c * (y_c @ wb[RWKV_WIDTH + CONV_WIDTH:]))
        x = x + rmsnorm(merged @ w_out[l], norm_mix_post[l])
        h = rmsnorm(x, norm_ffn_pre[l])
        gate, up = jnp.split(h @ w_ffn_in[l], 2, axis=-1)
        x = x + rmsnorm((jax.nn.silu(gate) * up) @ w_ffn_out[l], norm_ffn_post[l])
    return x


_drawn_inputs = setup_inputs


def setup_inputs(seed=0):
    import zlib

    import numpy as np

    out = dict(_drawn_inputs(seed))
    spreads = {}
    factors = {'rwkv_w_up': 6.137,
     'rwkv_k_k': 3.518,
     'rwkv_k_a': 2.676,
     'rwkv_ln_w': 2.98,
     'rwkv_ln_b': 8.0}
    for name, (base, spread) in spreads.items():
        noise = np.random.default_rng([zlib.crc32(name.encode()), seed]).standard_normal(out[name].shape)
        drawn = base * np.exp(spread * noise) if base else spread * noise
        out[name] = __import__('jax').numpy.asarray(drawn.astype(out[name].dtype))
    for name, factor in factors.items():
        out[name] = (out[name] * factor).astype(out[name].dtype)
    return out
```

```python
import math
from contextlib import ExitStack

import concourse.bass as bass
from concourse import mybir


def hybrid_layer(nc, x, norm_mix_pre, norm_mix_post, norm_ffn_pre, norm_ffn_post, w_in, rwkv_mu,
                 rwkv_w0, rwkv_w_up, rwkv_a0, rwkv_a_up, rwkv_g_up, rwkv_k_k, rwkv_k_a, rwkv_r_k,
                 rwkv_ln_w, rwkv_ln_b, conv_w, w_branch, w_out, w_ffn_in, w_ffn_out, out, spill):
    F = mybir.dt.float32
    R = mybir.dt.float32r
    I32 = mybir.dt.int32
    ALU = mybir.AluOpType
    ACT = mybir.ActivationFunctionType
    AX = mybir.AxisListType.X

    P = 128
    SEQ, D = x.shape[1], x.shape[2]
    NT = SEQ // P
    KT = D // P
    HD = 64
    NH = rwkv_r_k.shape[1]
    RW = NH * HD
    NJ = RW // P
    CW = conv_w.shape[2]
    CJ = CW // P
    HG, NG = 4, 3
    DILATION = (1, 4, 16)
    AJ = HG * NG * HD // P
    WINDOW = 128
    STRIDE = 4
    FT = w_ffn_out.shape[1] // P
    DFF = FT * P
    RT = rwkv_mu.shape[1] // P
    GATE0 = w_in.shape[2] - 3 * D
    PROJ_T = GATE0 // P
    CONV_T = 0
    ATT_T = RT + 3 * CJ
    SPILL_CONV, SPILL_ATT, SPILL_GATE = 0, 3 * CJ, PROJ_T - RT
    BT = 2 * NJ + 2
    NORM_EPS, GN_EPS = 1e-6, 64e-5
    DECAY = math.exp(-0.5)
    NEG = -3.0e38
    PAD = 2
    PITCH = SEQ + PAD
    LEVELS = 6

    SC = 256
    SLOT = KT * SC
    N_RWKV = RT * P // SC
    N_WIN = w_in.shape[2] // SC
    PER_T = 6
    S_REST = N_RWKV + NT * PER_T
    N_LEFT = N_WIN - S_REST
    N_MERGE, N_OUT, N_FIN, N_FOUT = D // SC, KT // 2, FT, FT // 2
    S_ATT = N_WIN
    S_MERGE = S_ATT + 1
    S_OUT = S_MERGE + N_MERGE
    S_FIN = S_OUT + N_OUT
    S_FOUT = S_FIN + N_FIN
    N_SLOTS = S_FOUT + N_FOUT

    C_MU = 0
    C_W0 = C_MU + RT
    C_A0 = C_W0 + NJ
    C_KK = C_A0 + NJ
    C_KA = C_KK + NJ
    C_RK = C_KA + NJ
    C_CONV = C_RK + NJ
    C_PRE = C_CONV + 3 * CJ
    C_FPRE = C_PRE + KT
    N_ROWS = C_FPRE + KT
    C_OMKA = 64
    S_X, S_Z, S_EPS = 0, 16, 60

    with ExitStack() as ctx:
        top = [(nc.sbuf_base + 63) // 64 * 64]

        def size(shape):
            return (4 * math.prod(shape[1:]) + 31) // 32 * 32

        def fixed(name, shape, dt=F):
            t = nc.alloc_sbuf_tensor_at(name, shape, dt, offset=top[0])
            top[0] += size(shape)
            return t

        w_raw = fixed("w_raw", [P, 2, SLOT])
        w_hi = fixed("w_hi", [P, 2, SLOT], R)
        w_lo = fixed("w_lo", [P, 2, SLOT], R)
        a_hi = fixed("a_hi", [P, KT, SEQ], R)
        a_lo = fixed("a_lo", [P, KT, SEQ], R)
        ident = fixed("ident", [P, P])
        causal = fixed("causal", [P, 2, P])
        chunk_run = fixed("chunk_run", [P, SEQ])
        head_rows = nc.alloc_sbuf_tensor_at("head_rows", [P, 2 * P], F, offset=top[0])
        level_mask = fixed("level_mask", [P, LEVELS, HD])
        head_ones = fixed("head_ones", [P, P])
        lora_up = fixed("lora_up", [P, RW])
        g_up = fixed("g_up", [P, RW])
        params = fixed("params", [P, 68])
        stat = fixed("stat", [P, 64])
        small = fixed("small", [P, 128])
        ARENA = top[0]

        def arena(name, shape, offset, dt=F):
            assert ARENA + offset + size(shape) <= nc.sbuf_usable_end, (name, offset)
            return nc.alloc_sbuf_tensor_at(name, shape, dt, offset=ARENA + offset), offset + size(shape)

        def up32(n):
            return (n + 31) // 32 * 32

        x_tok, o = arena("x_tok", [P, NT, D], 0)
        h_f32, o = arena("h_f32", [P, KT, SEQ], o)
        sq_x, o = arena("sq_x", [P, D], o)
        proj, AT_YC = arena("proj", [P, PROJ_T, PITCH], 0)
        AT_S = up32(RT * PITCH * 4)
        AT_C = up32((RT + CJ) * PITCH * 4)
        AT_Q = up32(ATT_T * PITCH * 4)
        y_c, AT_TAIL = arena("y_c", [P, 2, SEQ], AT_YC)
        param_rows, _ = arena("param_rows", [64, P], AT_TAIL + 5 * 4 * SEQ + 4096)
        PITCH4 = 4 * PITCH
        qk_sorted, o = arena("qk_sorted", [P, 2, 4, SEQ], AT_C)
        assert o <= AT_Q
        bias_win, o = arena("bias_win", [P, HG, 2 * P], AT_TAIL)
        bias_dil, AT_ROWS = arena("bias_dil", [P, (NG - 1) * HG, P], o)
        dist_i, o = arena("dist_i", [P, 2 * P], AT_ROWS, I32)
        rem_i, o = arena("rem_i", [P, 2 * P], o, I32)
        dist_f, o = arena("dist_f", [P, 2 * P], o)
        late_f, o = arena("late_f", [P, 2 * P], o)
        mask_f, o = arena("mask_f", [P, 2 * P], o)
        weights, o = arena("weights", [P, NG, SEQ], AT_ROWS)
        top_row, o = arena("top_row", [P, SEQ], o)
        p_buf, o = arena("p_buf", [P, 2, 2 * SEQ], up32((CONV_T + CJ) * PITCH4))
        pt_buf, o = arena("pt_buf", [P, 2, 2 * SEQ - P], o)
        assert o <= 3 * CJ * PITCH4
        o_win, o = arena("o_win", [P, 2, SEQ], up32((ATT_T + 2) * PITCH4))
        den, o = arena("den", [P, 2, SEQ], o)
        assert o <= (ATT_T + AJ) * PITCH4
        o_dil, o = arena("o_dil", [P, NG - 1, 2, SEQ], up32((ATT_T + AJ + 2) * PITCH4))
        assert o <= (ATT_T + 2 * AJ) * PITCH4
        spill_buf, o = arena("spill_buf", [P, 2, 2, SEQ], AT_S)
        assert o <= AT_C
        mt, o = arena("mt", [P, NH, 4, P], AT_C)
        assert o <= AT_Q
        xm, o = arena("xm", [P, RT, P], AT_Q)
        sig, e = arena("sig", [P, 2, NJ, P], o)
        wt, _ = arena("wt", [P, NH, P], o)
        cum, o = arena("cum", [P, NJ, P], e)
        tt, _ = arena("tt", [P, NH, P], e)
        prev, o = arena("prev", [P, NJ, P], o)
        ep, o = arena("ep", [P, NJ, P], o)
        kk, e = arena("kk", [P, NJ, P], o)
        qb, _ = arena("qb", [P, NH, HD], o)
        sq, o = arena("sq", [P, NJ, P], e)
        xs, _ = arena("xs", [P, NH, HD], e)
        k2, e = arena("k2", [P, NJ, P], o)
        us, _ = arena("us", [P, NH, HD], o)
        ar, o = arena("ar", [P, NJ, 2, P], e)
        bd, o = arena("bd", [P, NJ, P], o)
        kd, o = arena("kd", [P, NJ, P], o)
        b_tok, o = arena("b_tok", [P, NJ, P], o)
        v_tok, o = arena("v_tok", [P, NH, HD], o)
        assert o <= AT_YC, (o, AT_YC)
        rk, o = arena("rk", [P, NJ, P], AT_TAIL)
        k_tok, o = arena("k_tok", [P, NJ, P], o)
        state, o = arena("state", [P, NJ, 2, HD], o)
        g_tok, o = arena("g_tok", [P, NH, HD], o)
        y1, o = arena("y1", [P, NH, HD], o)
        y2, o = arena("y2", [P, NH, HD], o)
        ln_wb, o = arena("ln_wb", [P, 2, RW], o)
        y_a, o = arena("y_a", [P, NJ, SEQ], o)
        y_hi, o = arena("y_hi", [P, BT, SEQ], AT_C, R)
        y_lo, o = arena("y_lo", [P, BT, SEQ], o, R)
        merged, o = arena("merged", [P, KT, SEQ], o)
        g_att, _ = arena("g_att", [P, KT, SEQ], up32((CONV_T + CJ) * PITCH4))
        g_ab, o = arena("g_ab", [P, 2, 2, 2, SEQ], o)
        tmp, o = arena("tmp", [P, 2, SEQ], o)
        x_in, o = arena("x_in", [P, NT, D], AT_C)
        gain_mix, o = arena("gain_mix", [P, D], o)
        f_hi, o = arena("f_hi", [P, FT, SEQ], 0, R)
        f_lo, o = arena("f_lo", [P, FT, SEQ], o, R)
        x1, o = arena("x1", [P, NT, D], o)
        gain_ffn, o = arena("gain_ffn", [P, D], o)
        f_sig, e = arena("f_sig", [P, SEQ], o)
        f_act, e = arena("f_act", [P, SEQ], e)
        squares, _ = arena("squares", [P, D], o)
        row, e = arena("row", [P, D], e)
        h2_tok, o = arena("h2_tok", [P, NT, D], 0)
        h2_f32, o = arena("h2_f32", [P, KT, SEQ], o)

        ps = ctx.enter_context(nc.psum_tensor("ps", [P, 8, SEQ], F))

        class Signal:

            def __init__(self, name, per=1):
                self.sem, self.per = ctx.enter_context(nc.semaphore(name)), per

            def at(self, turn=0, k=0):
                return turn * self.per + k + 1

        def sem(name):
            return ctx.enter_context(nc.semaphore(name))

        raw_loaded = [sem("raw_loaded_even"), sem("raw_loaded_odd")]
        hi_ready, lo_ready, slot_used = sem("hi_ready"), sem("lo_ready"), sem("slot_used")
        x_loaded, rows_loaded, ups_loaded = [sem("x_loaded_0"), sem("x_loaded_1")], sem("rows_loaded"), sem("ups_loaded")
        ln_loaded, spilled = sem("ln_loaded"), [sem("spilled_even"), sem("spilled_odd")]
        qkv_loaded, conv_loaded = sem("qkv_loaded"), sem("conv_loaded")
        first_tile, spill_copied, dist_ready = sem("first_tile"), sem("spill_copied"), sem("dist_ready")
        g_att_ready, g_ab_ready = sem("g_att_ready"), sem("g_ab_ready")
        g_att_loaded, g_ab_loaded = sem("g_att_loaded"), [sem("g_ab_even"), sem("g_ab_odd")]
        xin_loaded, gains_loaded, out_stored = sem("xin_loaded"), sem("gains_loaded"), sem("out_stored")
        gain_ffn_loaded = sem("gain_ffn_loaded")
        dve_chain, act_chain, pool_chain = sem("dve_chain"), sem("act_chain"), sem("pool_chain")
        consts_ready, params_ready, rows_turned = sem("consts_ready"), sem("params_ready"), sem("rows_turned")
        eps_ready = sem("eps_ready")
        root_ready, rstd_ready, h_ready = sem("root_ready"), sem("rstd_ready"), sem("h_ready")
        turned, scaled, a_hi_ready, a_lo_ready = sem("turned"), sem("scaled"), sem("a_hi_ready"), sem("a_lo_ready")
        proj_out = sem("proj_out")
        v_turned, v_ready = sem("v_turned"), sem("v_ready")
        scores_done, scores_max, probs_ready = sem("scores_done"), sem("scores_max"), sem("probs_ready")
        probs_turned, probs_t_ready, pv_done = sem("probs_turned"), sem("probs_t_ready"), sem("pv_done")
        sorted_ready, o_ready, stats_turned = sem("sorted_ready"), sem("o_ready"), sem("stats_turned")
        mix_max, mix_exp, mix_den, spread = sem("mix_max"), sem("mix_exp"), sem("mix_den"), sem("spread")
        y_c_ready = sem("y_c_ready")
        xm_ready, lora_ready, z_done, g_done = Signal("xm_ready"), Signal("lora_ready"), Signal("z_done"), Signal("g_done")
        z_ready, sig_ready, sums_run, exps_ready = Signal("z_ready"), Signal("sig_ready"), Signal("sums_run"), Signal("exps_ready")
        kk_ready, sq_ready, ssq_done, ssq_ready = Signal("kk_ready"), Signal("sq_ready"), Signal("ssq_done"), Signal("ssq_ready")
        norm_ready, ops_ready, g_ready = Signal("norm_ready"), Signal("ops_ready"), Signal("g_ready")
        toks_done, toks_ready, bonus_done = Signal("toks_done"), Signal("toks_ready"), Signal("bonus_done")
        mt_done, mt_ready = Signal("mt_done", NH), Signal("mt_ready", NH)
        q_done, q_ready = Signal("q_done", LEVELS), Signal("q_ready", LEVELS)
        t_done, t_ready = Signal("t_done", LEVELS - 1), Signal("t_ready", LEVELS)
        w_done, w_ready = Signal("w_done", LEVELS), Signal("w_ready", LEVELS)
        x_done, x_ready = Signal("x_done", 2), Signal("x_ready", 2)
        u_done, u_ready = Signal("u_done", 2), Signal("u_ready", 2)
        s_done, s_ready = Signal("s_done", 2), Signal("s_ready", 2)
        y_done, y_mid, y_sq, y_var = Signal("y_done"), Signal("y_mid"), Signal("y_sq"), Signal("y_var")
        y_std, y_ready, y_turned, y_a_ready = Signal("y_std"), Signal("y_ready"), Signal("y_turned"), Signal("y_a_ready")
        state_zero = sem("state_zero")
        y_hi_ready, y_lo_ready = sem("y_hi_ready"), sem("y_lo_ready")
        att_tile_done = sem("att_tile_done")
        att_merged, pair_merged, merged_ready = sem("att_merged"), sem("pair_merged"), sem("merged_ready")
        z_tile_done, z_root, x1_ready = sem("z_tile_done"), sem("z_root"), sem("x1_ready")
        silu_sig, f_act_ready, f_hi_ready, f_lo_ready = sem("silu_sig"), sem("f_act_ready"), sem("f_hi_ready"), sem("f_lo_ready")
        row_ready = sem("row_ready")

        SPILLED = [16 * sum(1 for n in range(N_RWKV, N_WIN) if (n - N_RWKV) % 2 == b) for b in range(2)]

        block = ctx.enter_context(nc.Block())

        def cols(j0, n=1, lo=PAD, width=SEQ):
            return proj[:, j0:j0 + n, lo:lo + width]

        def q_row(gi, hh, which):
            rows, j = slice(HD * (hh % 2), HD * (hh % 2) + HD), hh // 2
            if gi == 0:
                return proj[rows, ATT_T + which * AJ + j, PAD:PAD + SEQ]
            return qk_sorted[rows, which, 2 * (gi - 1) + j]

        def sort_tokens(ap):
            return ap.rearrange("p (i r) -> p r i", r=STRIDE)

        def unsort(ap):
            return ap.rearrange("p (r i) -> p i r", r=STRIDE)

        def by_group(gi, ap):
            return ap if gi == 0 else unsort(ap)

        def token_blocks(ap):
            return ap.rearrange("p (i r) -> p i r", r=STRIDE)

        def over(ap, shape):
            return ap.unsqueeze(2).broadcast_to(shape)

        first_half = [lambda t, b=1 << l: t.rearrange("p h (n two b) -> p h n two b", two=2, b=b)[:, :, :, 0, :]
                      for l in range(LEVELS)]

        ATT_UNITS = [(gi, hh) for gi in range(NG) for hh in range(HG)]

        def blocks(gi):
            if gi == 0:
                return [(n, k) for n in range(NT) for k in range(max(0, n - 1), n + 1)]
            return [(r, r) for r in range(NT)]

        PART_ORDER = [*range(2 * NJ, BT), *range(2 * NJ)]

        top_of = lambda gi, t=slice(0, NT): small[:, 0:NG * NT * HG].rearrange("p (g t h) -> p g t h", g=NG, t=NT)[:, gi, t]
        sum_of = lambda gi, t=slice(0, NT): stat[:, 0:NG * NT * HG].rearrange("p (g t h) -> p g t h", g=NG, t=NT)[:, gi, t]
        less_top = lambda u: small[:, 48 + NT * (u % 2):48 + NT * (u % 2) + NT]

        class Chain:

            def __init__(self, eng, s):
                self.eng, self.sem, self.base, self.k, self.per, self.turn = eng, s, 0, 0, 0, 0

            def link(self, ins):
                self.k += 1
                ins.then_inc(self.sem, 1)
                self.eng.wait_ge(self.sem, self.turn * self.per + self.base + self.k)

            def loop(self, per):
                self.base, self.k, self.per = self.base + self.k, 0, per

            def begin(self, turn):
                self.turn, self.k = turn, 0

            def end(self, turns):
                assert self.k == self.per, (self.k, self.per)
                self.base, self.k, self.per, self.turn = self.base + self.per * turns, 0, 0, 0

        def passes(eng, body, count):
            body(0)
            if count > 1:
                with eng.Fori(1, count, 1) as i:
                    body(i)

        @block.sync
        def _(sp):
            wi = w_in[0].rearrange("(k p) (n c) -> n p k c", p=P, c=SC)
            wo = w_out[0].rearrange("(n k p) c -> n p k c", p=P, k=2)
            wb = w_branch[0].rearrange("(k p) c -> p k c", p=P)
            wf = w_ffn_in[0].rearrange("(k p) (half n c) -> half n p k c", p=P, c=P, half=2)
            wd = w_ffn_out[0].rearrange("(n k p) c -> n p k c", p=P, k=2)

            def load(n, parts):
                b = par(n)
                if not (isinstance(n, int) and n < 2):
                    sp.wait_ge(lo_ready, n - 1)
                for dst, src in parts:
                    sp.dma_start(dst, src).then_inc(raw_loaded[b], 16)

            def par(n):
                return par.b
            half8 = lambda b: w_raw[:, b].rearrange("p (k c) -> p k c", k=KT)
            half2 = lambda b: w_raw[:, b].rearrange("p (k c) -> p k c", k=2)

            sp.dma_start(x_tok[:, 0:2], x[0].rearrange("(t p) d -> p t d", p=P)[:, 0:2]).then_inc(x_loaded[0], 16)
            par.b = 0
            load(0, [(half8(0), wi[0])])
            sp.dma_start(x_tok[:, 2:4], x[0].rearrange("(t p) d -> p t d", p=P)[:, 2:4]).then_inc(x_loaded[1], 16)
            par.b = 1
            load(1, [(half8(1), wi[1])])
            wi2 = w_in[0].rearrange("(k p) (n two c) -> n two p k c", p=P, c=SC, two=2)
            with sp.Fori(1, S_REST // 2 + 1, 1) as i:
                for b in range(2):
                    par.b = b
                    load(i * 2 + b, [(half8(b), wi2[i, b])])
            sd = spill.rearrange("t p s -> p t s")
            sp.wait_ge(xm_ready.sem, NT)
            for b in range(2):
                sp.wait_ge(spilled[b], 16 * (3 * CJ // 4))
            sp.dma_start(cols(CONV_T, 3 * CJ), sd[:, SPILL_CONV:SPILL_CONV + 3 * CJ]).then_inc(conv_loaded, 16)
            par.b = (S_REST + 1) % 2
            load(S_REST + 1, [(half8(par.b), wi[S_REST + 1])])
            sp.wait_ge(y_a_ready.sem, NT)
            for b in range(2):
                sp.wait_ge(spilled[b], 16 * (NT * PER_T // 2))
            sp.dma_start(cols(ATT_T, 3 * AJ), sd[:, SPILL_ATT:SPILL_ATT + 3 * AJ]).then_inc(qkv_loaded, 16)
            for n in range(S_REST + 2, N_WIN):
                par.b = n % 2
                load(n, [(half8(par.b), wi[n])])
            par.b = S_ATT % 2
            load(S_ATT, [(half2(par.b), wb[:, 2 * NJ:BT, :])])
            for g in range(N_MERGE):
                par.b = (S_MERGE + g) % 2
                load(S_MERGE + g, [(half8(par.b), wb[:, 0:2 * NJ, g * SC:(g + 1) * SC])])
                if g == 0:
                    for b in range(2):
                        sp.wait_ge(spilled[b], SPILLED[b])
                    sp.wait_ge(pv_done, len(ATT_UNITS))
                    gate = [sd[:, SPILL_GATE + br * KT:SPILL_GATE + (br + 1) * KT] for br in range(3)]
                    sp.dma_start(g_att[:], gate[2]).then_inc(g_att_loaded, 16)
                    sp.wait_ge(y_lo_ready, 2)
                if g >= 2:
                    sp.wait_ge(pair_merged, g - 1)
                for br in range(2):
                    sp.dma_start(g_ab[:, g % 2, br], gate[br][:, 2 * g:2 * g + 2]).then_inc(g_ab_loaded[g % 2], 16)
            for m in range(N_OUT):
                par.b = (S_OUT + m) % 2
                load(S_OUT + m, [(half2(par.b), wo[m])])
            sp.wait_ge(slot_used, S_OUT)
            sp.wait_ge(pair_merged, N_MERGE)
            sp.dma_start(x_in[:], x[0].rearrange("(t p) d -> p t d", p=P)).then_inc(xin_loaded, 16)
            sp.dma_start(gain_mix[:], norm_mix_post.broadcast_to((P, D))).then_inc(gains_loaded, 16)
            sp.dma_start(gain_ffn[:], norm_ffn_post.broadcast_to((P, D))).then_inc(gain_ffn_loaded, 16)
            wf2 = w_ffn_in[0].rearrange("(k p) (half n two c) -> n two half p k c", p=P, c=P, half=2, two=2)
            with sp.Fori(0, N_FIN // 2, 1) as i:
                for b in range(2):
                    par.b = (S_FIN + b) % 2
                    dst = w_raw[:, par.b].rearrange("p (k half c) -> p k half c", k=KT, half=2)
                    load(i * 2 + (S_FIN + b), [(dst[:, :, 0], wf2[i, b, 0]), (dst[:, :, 1], wf2[i, b, 1])])
            for m in range(N_FOUT):
                par.b = (S_FOUT + m) % 2
                load(S_FOUT + m, [(half2(par.b), wd[m])])
            sp.wait_ge(out_stored, 16 * NT)

        def raw_value(n, i=None, stride=2):
            extra = sum(1 for m in range(S_FIN, min(n + 1, S_FOUT)) if m % 2 == n % 2)
            value = 16 * (n // 2 + 1 + extra)
            if i is None:
                return value
            return i * (stride // 2 * (32 if n >= S_FIN else 16)) + value

        @block.gpsimd
        def _(pool):
            g = nc.gpsimd
            ch = Chain(pool, pool_chain)
            link = ch.link
            link(g.memset(level_mask[:], 1.0))
            link(g.memset(causal[:], 1.0))
            link(g.memset(head_ones[:], 0.0))
            link(g.memset(chunk_run[:], 1.0))
            link(g.memset(ident[:], 0.0))
            link(g.affine_select(out=ident[:], in_=ident[:], compare_op=ALU.not_equal, fill=1.0, base=0,
                            pattern=[[-1, P]], channel_multiplier=1))
            for half in range(2):
                rows = slice(HD * half, HD * half + HD)
                link(g.memset(head_ones[rows, rows], 1.0))
            link(g.memset(chunk_run[:].rearrange("p (n c) -> p n c", c=HD)[:, :, 0:1], 0.0))
            for inclusive in range(2):
                link(g.affine_select(out=causal[:, inclusive], in_=causal[:, inclusive], compare_op=ALU.is_gt,
                                fill=0.0, base=inclusive, pattern=[[1, P]], channel_multiplier=-1))
            for lv in range(LEVELS):
                b = 1 << lv
                nb = HD // b
                m = level_mask[:, lv].rearrange("p (n b) -> p n b", b=b)
                link(g.affine_select(out=m, in_=m, compare_op=ALU.is_ge, fill=0.0, base=-b,
                                pattern=[[-2 * b, nb], [0, b]], channel_multiplier=1))
            for lv in range(LEVELS):
                b = 1 << lv
                nb = HD // b
                m = level_mask[:, lv].rearrange("p (n b) -> p n b", b=b)
                link(g.affine_select(out=m, in_=m, compare_op=ALU.is_ge, fill=0.0, base=2 * b - 1,
                                pattern=[[2 * b, nb], [0, b]], channel_multiplier=-1))
            g.memset(causal[0:HD, :, HD:P], 0.0).then_inc(consts_ready, 1)

            def low(n, b):
                pool.wait_ge(hi_ready, n + 1)
                g.tensor_tensor(w_lo[:, b], w_raw[:, b], w_hi[:, b].bitcast(F), ALU.subtract).then_inc(lo_ready, 1)

            with pool.Fori(0, S_REST // 2 + 1, 1) as i:
                for b in range(2):
                    low(i * 2 + b, b)
            pool.wait_ge(y_a_ready.sem, NT)
            g.iota(dist_i[:], [[-1, 2 * P]], base=P, channel_multiplier=1).then_inc(dist_ready, 1)
            link(g.memset(head_rows[:], 1.0))
            link(g.affine_select(out=head_rows[:], in_=head_rows[:], compare_op=ALU.is_ge, fill=0.0, base=0,
                                 pattern=[[1, 2 * P]], channel_multiplier=-HD))
            g.affine_select(out=head_rows[:], in_=head_rows[:], compare_op=ALU.is_ge, fill=0.0, base=HD - 1,
                                 pattern=[[-1, 2 * P]], channel_multiplier=HD).then_inc(dist_ready, 1)
            with pool.Fori(S_REST // 2 + 1, N_SLOTS // 2, 1) as i:
                for b in range(2):
                    low(i * 2 + b, b)

        @block.scalar
        def _(act):
            s = nc.scalar
            ch = Chain(act, act_chain)
            link = ch.link

            def high(n, loaded, b):
                act.wait_ge(raw_loaded[b], loaded)
                if not (isinstance(n, int) and n < 2):
                    act.wait_ge(slot_used, n - 1)
                s.copy(w_hi[:, b], w_raw[:, b]).then_inc(hi_ready, 1)

            def root_mean_square(src, junk, c, done):
                link(s.activation(junk, src, ACT.Square, accum_out=stat[:, c:c + 1]))
                s.activation(stat[:, c:c + 1], stat[:, c:c + 1], ACT.Sqrt, bias=stat[:, S_EPS:S_EPS + 1],
                             scale=1.0 / D).then_inc(done, 1)

            def z_root_of(t, turn, slots):
                if t < NT - 1:
                    act.wait_ge(z_tile_done, turn * (NT - 1) + t + 1)
                else:
                    act.wait_ge(slot_used, slots)
                root_mean_square(ps[:, 2 * t:2 * t + 2].rearrange("p a b -> p (a b)"), squares[:], S_Z + t, z_root)

            def normed(turn, src, dst, f32, junk, ready, ahead):
                lag = 1 if turn else 0
                for i in range(NT + 2):
                    ahead(i)
                    j = i - lag
                    if 0 <= j < NT:
                        ready(j)
                        root_mean_square(src[:, j], junk, S_X + j, root_ready)
                        act.wait_ge(rstd_ready, turn * NT + j + 1)
                        s.activation(dst[:, j], src[:, j], ACT.Copy, scale=stat[:, S_X + j:S_X + j + 1]).then_inc(h_ready, 1)
                    if i >= 2:
                        c = slice((i - 2) * P, (i - 1) * P)
                        act.wait_ge(scaled, turn * NT + i - 1)
                        s.copy(a_hi[:, :, c], f32[:, :, c]).then_inc(a_hi_ready, 1)

            rows = [(rwkv_mu[0], RT, C_MU), (rwkv_w0[0], NJ, C_W0), (rwkv_a0[0], NJ, C_A0), (rwkv_k_k[0], NJ, C_KK),
                    (rwkv_k_a[0], NJ, C_KA), (norm_mix_pre[0], KT, C_PRE), (norm_ffn_pre[0], KT, C_FPRE)]
            for src, n, c in rows:
                act.dma_start(param_rows[c:c + n, :], src.rearrange("(a b) -> a b", b=P)).then_inc(rows_loaded, 16)
            act.dma_start(param_rows[C_RK:C_RK + NJ, :], rwkv_r_k[0].rearrange("(a b) c -> a (b c)", b=2)).then_inc(rows_loaded, 16)
            act.dma_start(param_rows[C_CONV:C_CONV + 3 * CJ, :],
                          conv_w[0].rearrange("k (a b) -> (k a) b", b=P)).then_inc(rows_loaded, 16)
            act.dma_start(lora_up[0:HD, :], rwkv_w_up[0]).then_inc(ups_loaded, 16)
            act.dma_start(lora_up[HD:P, :], rwkv_a_up[0]).then_inc(ups_loaded, 16)
            act.dma_start(g_up[:], rwkv_g_up[0]).then_inc(ups_loaded, 16)

            act.wait_ge(eps_ready, 1)
            normed(0, x_tok, x_tok, h_f32, sq_x[:], lambda j: act.wait_ge(x_loaded[j // 2], 16),
                   lambda i: high(0, raw_value(0), 0) if i == 2 else None)
            high(1, raw_value(1), 1)
            act.wait_ge(params_ready, 1)
            act.dma_start(ln_wb[:, 0], rwkv_ln_w.broadcast_to((P, RW))).then_inc(ln_loaded, 16)
            act.dma_start(ln_wb[:, 1], rwkv_ln_b.broadcast_to((P, RW))).then_inc(ln_loaded, 16)
            for n in range(2, N_RWKV + 2):
                high(n, raw_value(n), n % 2)

            beside = spill[0:2 * NT * PER_T].rearrange("(i k two) p s -> i k p two s", k=PER_T, two=2)

            def rwkv(T):
                def need(sig_, k=0):
                    act.wait_ge(sig_.sem, sig_.at(T, k))

                def evacuate(q):
                    k, half = q // 2, q % 2
                    b = k % 2
                    if half == 0:
                        act.wait_ge(first_tile, T * PER_T + (k + 1))
                        if not (isinstance(T, int) and k < 2):
                            act.wait_ge(spilled[b], T * (8 * PER_T) + 16 * (k // 2))
                    else:
                        act.wait_ge(slot_used, T * PER_T + (N_RWKV + k + 1))
                    s.copy(spill_buf[:, b, half], ps[:, 6 + half]).then_inc(spill_copied, 1)
                    if half == 1:
                        act.wait_ge(spill_copied, T * (2 * PER_T) + (q + 1))
                        act.dma_start(beside[T, k], spill_buf[:, b]).then_inc(spilled[b], 16)
                        n = N_RWKV + k + 2
                        high(T * PER_T + n, raw_value(n, T, PER_T), n % 2)

                need(xm_ready)
                s.activation(xm[0:HD, RT - 2], xm[0:HD, RT - 2], ACT.Tanh)
                s.activation(xm[:, RT - 1], xm[:, RT - 1], ACT.Sigmoid).then_inc(lora_ready.sem, 1)
                need(kk_ready)
                s.activation(sq[:], kk[:], ACT.Square).then_inc(sq_ready.sem, 1)
                evacuate(0)
                need(z_ready)
                s.activation(sig[:], sig[:], ACT.Sigmoid).then_inc(sig_ready.sem, 1)
                need(g_done)
                s.copy(g_tok[:], ps[:, 2].rearrange("p (h c) -> p h c", h=NH)).then_inc(g_ready.sem, 1)
                evacuate(1)
                need(sums_run)
                s.activation(ep[:], cum[:], ACT.Exp, scale=-DECAY)
                s.activation(prev[:], prev[:], ACT.Exp, scale=-DECAY)
                s.activation(cum[:], cum[:], ACT.Exp, scale=DECAY).then_inc(exps_ready.sem, 1)
                evacuate(2)
                need(ssq_ready)
                s.activation(sq[:], sq[:], ACT.Sqrt).then_inc(norm_ready.sem, 1)
                for q in (3, 4, 5):
                    evacuate(q)
                need(toks_done)
                s.copy(b_tok[:], ps[:, 4].rearrange("p (h c) -> p h c", h=NJ))
                s.copy(k_tok[:], ps[:, 5].rearrange("p (h c) -> p h c", h=NJ))
                s.copy(v_tok[:], ps[:, 0].rearrange("p (h c) -> p h c", h=NH)).then_inc(toks_ready.sem, 1)
                for lv in range(LEVELS):
                    need(w_done, lv)
                    s.copy(wt[:], ps[:, 3:5].rearrange("p a (h t) -> p (a h) t", t=P)).then_inc(w_ready.sem, 1)
                    if lv in (2, 4):
                        evacuate(5 + lv // 2)
                for c in range(2):
                    r = slice(HD * c, HD * c + HD)
                    need(x_done, c)
                    s.copy(xs[r], ps[r, 4].rearrange("p (h v) -> p h v", h=NH)).then_inc(x_ready.sem, 1)
                    need(u_done, c)
                    s.copy(us[r], ps[r, 1].rearrange("p (h v) -> p h v", h=NH)).then_inc(u_ready.sem, 1)
                    if c == 0:
                        evacuate(8)
                need(y_mid)
                s.activation(y2[:], y1[:], ACT.Square).then_inc(y_sq.sem, 1)
                evacuate(9)
                need(y_var)
                s.activation(small[:, 48:48 + NH], small[:, 48:48 + NH], ACT.Sqrt).then_inc(y_std.sem, 1)
                evacuate(10)
                evacuate(11)
                need(y_turned)
                dst = y_a[:].rearrange("p j (t c) -> p j t c", c=P)
                s.copy(dst[:, :, T], ps[:, 0].rearrange("p (j c) -> p j c", j=NJ)).then_inc(y_a_ready.sem, 1)

            act.wait_ge(state_zero, 1)
            passes(act, rwkv, NT)

            left = spill[2 * NT * PER_T:].rearrange("(n two) p s -> n p two s", two=2)

            def keep(m, bank):
                n, b = S_REST + m, (S_REST - N_RWKV + m) % 2
                act.wait_ge(slot_used, n + 1)
                act.wait_ge(spilled[b], 16 * ((n - N_RWKV) // 2))
                s.copy(spill_buf[:, b], ps[:, bank:bank + 2]).then_inc(spill_copied, 2)
                act.wait_ge(spill_copied, 2 * (n - N_RWKV) + 2)
                act.dma_start(left[m], spill_buf[:, b]).then_inc(spilled[b], 16)
                high(n + 2, raw_value(n + 2), n % 2)

            for m in range(N_LEFT - 1):
                keep(m, 2 * (m % 2))
            act.wait_ge(qkv_loaded, 16)
            for which in range(2):
                for j in range(4):
                    s.copy(qk_sorted[:, which, j].rearrange("p (r i) -> p r i", r=STRIDE),
                           sort_tokens(cols(ATT_T + which * AJ + 2 + j)[:, 0])).then_inc(sorted_ready, 1)

            n_units = len(ATT_UNITS)
            for u in range(n_units + 1):
                if u < n_units:
                    gi, hh = ATT_UNITS[u]
                    act.wait_ge(scores_max, u + 1)
                    for t in range(NT):
                        if gi == 0:
                            c = slice(2 * P * t + (P if t == 0 else 0), 2 * P * (t + 1))
                        else:
                            c = slice(P * t, P * (t + 1))
                        last = s.activation(p_buf[:, u % 2, c], p_buf[:, u % 2, c], ACT.Exp, bias=less_top(u)[:, t:t + 1],
                                            accum_out=sum_of(gi, t)[:, hh:hh + 1])
                    last.then_inc(probs_ready, 1)
                if u > 0:
                    w = u - 1
                    act.wait_ge(probs_turned, w + 1)
                    if w >= 2:
                        act.wait_ge(pv_done, w - 1)
                    if ATT_UNITS[w][0] == 0:
                        s.copy(pt_buf[:, w % 2], ps[:, 4:6].rearrange("p a b -> p (a b)")[:, 0:2 * SEQ - P]).then_inc(probs_t_ready, 1)
                    else:
                        s.copy(pt_buf[:, w % 2, 0:SEQ], ps[:, 4 + w % 2]).then_inc(probs_t_ready, 1)
            act.wait_ge(mix_max, 1)
            s.activation(weights[0:HG], weights[0:HG], ACT.Exp).then_inc(mix_exp, 1)
            keep(N_LEFT - 1, 6)

            def y_part(t):
                return y_a[:, t] if t < NJ else cols(CONV_T + t - NJ)[:, 0] if t < 2 * NJ else y_c[:, t - 2 * NJ]

            act.wait_ge(y_c_ready, 1)
            act.wait_ge(y_a_ready.sem, NT)
            for t in PART_ORDER:
                s.copy(y_hi[:, t], y_part(t)).then_inc(y_hi_ready, 1)
            high(S_ATT + 2, raw_value(S_ATT + 2), (S_ATT + 2) % 2)

            def gates(g):
                act.wait_ge(g_ab_loaded[g % 2], 32 * (g // 2 + 1))
                s.activation(g_ab[:, g % 2], g_ab[:, g % 2], ACT.Sigmoid).then_inc(g_ab_ready, 1)

            act.wait_ge(g_att_loaded, 16)
            s.activation(g_att[:], g_att[:], ACT.Sigmoid).then_inc(g_att_ready, 1)
            gates(0)
            gates(1)
            for g in range(N_MERGE):
                high(S_MERGE + g + 2, raw_value(S_MERGE + g + 2), (S_MERGE + g) % 2)
                act.wait_ge(pair_merged, g + 1)
                s.copy(a_hi[:, 2 * g:2 * g + 2], merged[:, 2 * g:2 * g + 2]).then_inc(merged_ready, 1)
                if g + 2 < N_MERGE:
                    gates(g + 2)

            for m in range(N_OUT - 1):
                high(S_OUT + m + 2, raw_value(S_OUT + m + 2), (S_OUT + m) % 2)

            normed(1, x1, h2_tok, h2_f32, squares[:], lambda j: act.wait_ge(x1_ready, j + 1),
                   lambda i: z_root_of(i, 0, S_FIN) if i < NT else None)
            high(S_FIN + 1, raw_value(S_FIN + 1), (S_FIN + 1) % 2)

            def ffn_in(i):
                for b in range(2):
                    n = i * 2 + b
                    act.wait_ge(slot_used, n + S_FIN + 1)
                    s.activation(f_sig[:], ps[:, (S_FIN + b) % 2 * 2], ACT.Sigmoid).then_inc(silu_sig, 1)
                    high(n + S_FIN + 2, raw_value(S_FIN + 2 + b, i) if not isinstance(i, int) else raw_value(S_FIN + 2 + b + 2 * i),
                         (S_FIN + b) % 2)
                    act.wait_ge(f_act_ready, n + 1)
                    dst = f_hi[:].rearrange("p (n two) t -> p n two t", two=2)
                    s.copy(dst[:, i, b], f_act[:]).then_inc(f_hi_ready, 1)

            with act.Fori(0, N_FIN // 2 - 1, 1) as i:
                ffn_in(i)
            ffn_in(N_FIN // 2 - 1)
            for m in range(N_FOUT - 2):
                high(S_FOUT + m + 2, raw_value(S_FOUT + m + 2), (S_FOUT + m) % 2)
            for t in range(NT + 1):
                if t < NT:
                    z_root_of(t, 1, N_SLOTS)
                if t > 0:
                    act.wait_ge(row_ready, t)
                    act.dma_start(out[0].rearrange("(t p) d -> t p d", p=P)[t - 1], x1[:, t - 1]).then_inc(out_stored, 16)

        @block.vector
        def _(dve):
            v = nc.vector
            ch = Chain(dve, dve_chain)
            link = ch.link

            def recip_root(root, value, c, done=None):
                dve.wait_ge(root, value)
                last = v.reciprocal(stat[:, c:c + 1], stat[:, c:c + 1])
                link(last) if done is None else last.then_inc(done, 1)

            def add_normed(t, turn, xin, gain, dst, done):
                recip_root(z_root, turn * NT + t + 1, S_Z + t)
                link(v.scalar_tensor_tensor(out=row[:], in0=ps[:, 2 * t:2 * t + 2].rearrange("p a b -> p (a b)"),
                                            scalar=stat[:, S_Z + t:S_Z + t + 1], in1=gain[:], op0=ALU.mult, op1=ALU.mult))
                v.tensor_tensor(dst[:, t], xin[:, t], row[:], ALU.add).then_inc(done, 1)
                dve.wait_ge(done, t + 1)

            def normed(turn, c_gain, f32, base, ahead):
                lag = 1 if turn else 0
                for i in range(NT + 2):
                    j = i - lag
                    if 0 <= j < NT:
                        recip_root(root_ready, turn * NT + j + 1, S_X + j, rstd_ready)
                    ahead(i)
                    if 1 <= i <= NT:
                        t = i - 1
                        dve.wait_ge(turned, turn * NT + t + 1)
                        v.tensor_tensor(f32[:, :, t * P:(t + 1) * P],
                                        ps[:, 2 * t:2 * t + 2].rearrange("p a (b c) -> p (a b) c", c=P),
                                        over(params[:, c_gain:c_gain + KT], (P, KT, P)), ALU.mult).then_inc(scaled, 1)
                    if i >= 2:
                        c = slice((i - 2) * P, (i - 1) * P)
                        dve.wait_ge(a_hi_ready, turn * NT + i - 1)
                        v.tensor_tensor(a_lo[:, :, c], f32[:, :, c], a_hi[:, :, c].bitcast(F), ALU.subtract).then_inc(a_lo_ready, 1)

            v.memset(stat[:, S_EPS:S_EPS + 1], NORM_EPS).then_inc(eps_ready, 1)
            dve.wait_ge(rows_turned, 1)
            link(v.tensor_copy(params[:, 0:N_ROWS], ps[:, 7, 0:N_ROWS]))
            v.tensor_scalar(params[:, C_OMKA:C_OMKA + NJ], params[:, C_KA:C_KA + NJ], -1.0, 1.0, ALU.mult, ALU.add).then_inc(params_ready, 1)
            normed(0, C_PRE, h_f32, 0, lambda i: None)
            dve.wait_ge(a_lo_ready, NT)
            link(v.memset(proj[:, 0:RT, 0:PAD], 0.0))

            for n in range(N_RWKV):
                dve.wait_ge(slot_used, n + 1)
                v.tensor_copy(cols(2 * n, 2), ps[:, 2 * (n % 2):2 * (n % 2) + 2]).then_inc(proj_out, 1)
            dve.wait_ge(proj_out, N_RWKV)

            dve.wait_ge(consts_ready, 1)
            v.memset(state[:], 0.0).then_inc(state_zero, 1)
            dve.wait_ge(state_zero, 1)
            dve.wait_ge(ln_loaded, 32)

            def rwkv(T):
                def need(sig_, k=0):
                    dve.wait_ge(sig_.sem, sig_.at(T, k))

                r_, k_, v_ = xm[:, 0:NJ], xm[:, NJ:2 * NJ], xm[:, 2 * NJ:3 * NJ]
                four = (P, NJ, P)

                def par(c, n=NJ):
                    return over(params[:, c:c + n], (P, n, P))

                now = proj[:, 0:RT, PAD:PITCH].rearrange("p j (t c) -> p j t c", c=P)[:, :, T]
                before = proj[:, 0:RT, PAD - 1:PITCH - 1].rearrange("p j (t c) -> p j t c", c=P)[:, :, T]
                link(v.tensor_tensor(xm[:], before, now, ALU.subtract))
                link(v.tensor_tensor(xm[:], xm[:], par(C_MU, RT), ALU.mult))
                v.tensor_tensor(xm[:], xm[:], now, ALU.add).then_inc(xm_ready.sem, 1)
                need(xm_ready)
                v.tensor_tensor(kk[:], k_, par(C_KK), ALU.mult).then_inc(kk_ready.sem, 1)
                need(z_done)
                v.tensor_tensor(sig[:, 0], ps[:, 0].rearrange("p (j t) -> p j t", j=NJ), par(C_W0), ALU.add)
                v.tensor_tensor(sig[:, 1], ps[:, 1].rearrange("p (j t) -> p j t", j=NJ), par(C_A0), ALU.add).then_inc(z_ready.sem, 1)
                need(ssq_done)
                need(sq_ready)
                v.tensor_scalar(sq[:], ps[:, 3].rearrange("p (j t) -> p j t", j=NJ), 1e-12, None, ALU.max).then_inc(ssq_ready.sem, 1)
                need(sig_ready)
                link(v.tensor_tensor_scan(cum[:].rearrange("p j t -> p (j t)"), chunk_run[:],
                                          sig[:, 0].rearrange("p j t -> p (j t)"), 0.0, ALU.mult, ALU.add))
                v.tensor_tensor(prev[:], cum[:], sig[:, 0], ALU.subtract).then_inc(sums_run.sem, 1)
                link(v.tensor_tensor(k2[:], sig[:, 1], par(C_KA), ALU.mult))
                link(v.tensor_tensor(k2[:], k2[:], par(C_OMKA), ALU.add))
                link(v.tensor_tensor(k2[:], k2[:], k_, ALU.mult))
                link(v.tensor_tensor(rk[:], r_, k2[:], ALU.mult))
                link(v.tensor_tensor(rk[:], rk[:], par(C_RK), ALU.mult))
                need(norm_ready)
                link(v.reciprocal(sq[:], sq[:]))
                link(v.tensor_tensor(kk[:], kk[:], sq[:], ALU.mult))
                link(v.tensor_tensor(bd[:], kk[:], sig[:, 1], ALU.mult))
                need(exps_ready)
                v.tensor_tensor(ar[:, :, 1], r_, ep[:], ALU.mult)
                v.tensor_tensor(kd[:], k2[:], cum[:], ALU.mult)
                v.tensor_tensor(bd[:], bd[:], cum[:], ALU.mult)
                ends = ep[:].rearrange("p j (c t) -> p c j t", t=HD)[:, :, :, HD - 1:HD]
                for c in range(2):
                    v.tensor_tensor(small[:, 64 + 8 * c:72 + 8 * c].rearrange("p (j h) -> p j h", h=2),
                                    ends[:, c].broadcast_to((P, NJ, 2)),
                                    head_ones[:, ::HD].unsqueeze(1).broadcast_to((P, NJ, 2)), ALU.mult)
                v.scalar_tensor_tensor(out=ar[:, :, 0], in0=kk[:], scalar=-1.0, in1=prev[:], op0=ALU.mult,
                                       op1=ALU.mult).then_inc(ops_ready.sem, 1)
                need(ops_ready)
                link(v.tensor_copy(tt[:], ident[:].unsqueeze(1).broadcast_to((P, NH, P))))
                for h in range(NH):
                    need(mt_done, h)
                    v.tensor_tensor(mt[:, h].rearrange("p (a b) t -> p a b t", a=2),
                                    ps[:, 1 + h % 3].rearrange("p (a b t) -> p a b t", a=2, b=2),
                                    causal[:].unsqueeze(1).broadcast_to((P, 2, 2, P)), ALU.mult).then_inc(mt_ready.sem, 1)
                need(bonus_done)
                link(v.tensor_copy(small[:, 56:56 + NH], ps[:, 5, 0:NH]))
                for lv in range(LEVELS):
                    need(q_done, lv)
                    v.tensor_tensor(qb[:], ps[:, 0].rearrange("p (h c) -> p h c", h=NH),
                                    level_mask[:, lv].unsqueeze(1).broadcast_to((P, NH, HD)), ALU.mult).then_inc(q_ready.sem, 1)
                    dst = first_half[lv](tt[:])
                    if lv == 0:
                        need(q_ready, 0)
                        add = qb[:].rearrange("p h (n b) -> p h n b", b=1)
                    else:
                        need(t_done, lv - 1)
                        need(w_done, lv - 1)
                        add = ps[:, 1].rearrange("p (h n b) -> p h n b", h=NH, b=1 << lv)
                    hn = "p h n b -> p (h n) b"
                    v.tensor_tensor(dst.rearrange(hn), dst.rearrange(hn), add.rearrange(hn), ALU.add).then_inc(t_ready.sem, 1)
                for c in range(2):
                    need(s_done, c)
                    link(v.tensor_tensor(state[:], state[:], ps[:, 2].rearrange("p (j h v) -> p j h v", j=NJ, h=2), ALU.add))
                    st = state[:].rearrange("p j h v -> p (j h) v")
                    v.tensor_tensor(st, st, over(small[:, 64 + 8 * c:72 + 8 * c], (P, NH, HD)), ALU.mult).then_inc(s_ready.sem, 1)
                need(y_done)
                y_ps = ps[:, 5].rearrange("p (h v) -> p h v", h=NH)
                full = (P, NH, HD)
                link(v.tensor_reduce(small[:, 40:40 + NH], y_ps, AX, ALU.add))
                link(v.tensor_scalar(small[:, 40:40 + NH], small[:, 40:40 + NH], 1.0 / HD, None, ALU.mult))
                v.tensor_tensor(y1[:], y_ps, over(small[:, 40:40 + NH], full), ALU.subtract).then_inc(y_mid.sem, 1)
                need(y_sq)
                link(v.tensor_reduce(small[:, 48:48 + NH], y2[:], AX, ALU.add))
                v.tensor_scalar(small[:, 48:48 + NH], small[:, 48:48 + NH], 1.0 / HD, GN_EPS, ALU.mult, ALU.add).then_inc(y_var.sem, 1)
                link(v.tensor_tensor(y2[:], v_tok[:], over(small[:, 56:56 + NH], full), ALU.mult))
                need(y_std)
                link(v.reciprocal(small[:, 48:48 + NH], small[:, 48:48 + NH]))
                link(v.tensor_tensor(y1[:], y1[:], over(small[:, 48:48 + NH], full), ALU.mult))
                lnw = [ln_wb[:, k].rearrange("p (h v) -> p h v", h=NH) for k in range(2)]
                link(v.tensor_tensor(y1[:], y1[:], lnw[0], ALU.mult))
                link(v.tensor_tensor(y1[:], y1[:], lnw[1], ALU.add))
                link(v.tensor_tensor(y1[:], y1[:], y2[:], ALU.add))
                need(g_ready)
                v.tensor_tensor(y1[:], y1[:], g_tok[:], ALU.mult).then_inc(y_ready.sem, 1)
                need(y_ready)

            ch.loop(24)

            def rwkv_pass(T):
                ch.begin(T)
                rwkv(T)

            passes(dve, rwkv_pass, NT)
            ch.end(NT)

            dve.wait_ge(dist_ready, 1)
            dve.wait_ge(y_a_ready.sem, NT)
            link(v.tensor_copy(dist_f[:], dist_i[:]))
            link(v.tensor_scalar(rem_i[:], dist_i[:], DILATION[2] // STRIDE - 1, None, ALU.bitwise_and))
            link(v.tensor_scalar(late_f[:], dist_f[:], 0.0, NEG, ALU.is_lt, ALU.mult))
            slope = [2.0 ** (-8.0 * (a + 1) / (HG * NG)) for a in range(HG * NG)]
            link(v.tensor_scalar(mask_f[:], dist_f[:], float(WINDOW), NEG, ALU.is_gt, ALU.mult))
            link(v.tensor_tensor(mask_f[:], mask_f[:], late_f[:], ALU.min))
            for hh in range(HG):
                last = v.scalar_tensor_tensor(out=bias_win[:, hh], in0=dist_f[:], scalar=-slope[hh],
                                              in1=mask_f[:], op0=ALU.mult, op1=ALU.add)
            link(last)
            link(v.tensor_copy(mask_f[:], rem_i[:]))
            link(v.tensor_scalar(mask_f[:], mask_f[:], 0.0, NEG, ALU.is_gt, ALU.mult))
            link(v.tensor_tensor(mask_f[:], mask_f[:], late_f[:], ALU.min))
            for gi in range(1, NG):
                mask = late_f if DILATION[gi] == STRIDE else mask_f
                for hh in range(HG):
                    last = v.scalar_tensor_tensor(out=bias_dil[:, (gi - 1) * HG + hh], in0=dist_f[:, P:2 * P],
                                                  scalar=-STRIDE * slope[gi * HG + hh], in1=mask[:, P:2 * P],
                                                  op0=ALU.mult, op1=ALU.add)
            link(last)

            dve.wait_ge(conv_loaded, 16)
            B0, C0, X0 = CONV_T, CONV_T + CJ, CONV_T + 2 * CJ
            link(v.tensor_tensor(cols(C0, CJ), cols(C0, CJ), cols(X0, CJ), ALU.mult))
            for t in range(CJ):
                tap = [params[:, C_CONV + k * CJ + t:C_CONV + k * CJ + t + 1] for k in range(3)]
                last = v.tensor_scalar(cols(X0 + t)[:, 0], proj[:, C0 + t, 0:SEQ], tap[0], None, ALU.mult)
            link(last)
            for k in range(1, 3):
                for t in range(CJ):
                    tap = params[:, C_CONV + k * CJ + t:C_CONV + k * CJ + t + 1]
                    last = v.scalar_tensor_tensor(out=cols(X0 + t)[:, 0], in0=proj[:, C0 + t, k:k + SEQ], scalar=tap,
                                                  in1=cols(X0 + t)[:, 0], op0=ALU.mult, op1=ALU.add)
                link(last)
            link(v.tensor_tensor(cols(B0, CJ), cols(B0, CJ), cols(X0, CJ), ALU.mult))

            for t in range(AJ):
                dve.wait_ge(v_turned, t + 1)
                v.tensor_copy(cols(ATT_T + 2 * AJ + t)[:, 0], ps[:, t]).then_inc(v_ready, 1)
            dve.wait_ge(sorted_ready, 8)

            def keep_output(p):
                dve.wait_ge(pv_done, 2 * p + 2)
                gi, j = p // 2, p % 2
                if gi == 0:
                    v.tensor_copy(o_win[:, j], ps[:, 6 + p % 2]).then_inc(o_ready, 1)
                else:
                    v.tensor_copy(token_blocks(o_dil[:, gi - 1, j]), unsort(ps[:, 6 + p % 2])).then_inc(o_ready, 1)

            for u, (gi, hh) in enumerate(ATT_UNITS):
                dve.wait_ge(scores_done, u + 1)
                if u >= 2:
                    dve.wait_ge(probs_turned, u - 1)
                sb = 2 * (u % 2)
                top = top_of(gi)[:, :, hh]
                if gi == 0:
                    sc = ps[:, sb:sb + 2].rearrange("p a (b c) -> p (a b) c", c=2 * P)
                    pb = p_buf[:, u % 2].rearrange("p (n c) -> p n c", c=2 * P)
                    v.scalar_tensor_tensor(out=pb[:, 0, P:2 * P], in0=sc[:, 0, P:2 * P], scalar=HD ** -0.5,
                                           in1=bias_win[:, hh, P:2 * P], op0=ALU.mult, op1=ALU.add)
                    link(v.scalar_tensor_tensor(out=pb[:, 1:NT], in0=sc[:, 1:NT], scalar=HD ** -0.5,
                                                in1=bias_win[:, hh].unsqueeze(1).broadcast_to((P, NT - 1, 2 * P)),
                                                op0=ALU.mult, op1=ALU.add))
                    v.tensor_reduce(top[:, 0:1], pb[:, 0, P:2 * P], AX, ALU.max)
                    link(v.tensor_reduce(top[:, 1:NT], pb[:, 1:NT], AX, ALU.max))
                else:
                    pb = p_buf[:, u % 2, 0:SEQ].rearrange("p (n c) -> p n c", c=P)
                    link(v.scalar_tensor_tensor(out=pb, in0=ps[:, sb].rearrange("p (n c) -> p n c", c=P), scalar=HD ** -0.5,
                                                in1=bias_dil[:, (gi - 1) * HG + hh].unsqueeze(1).broadcast_to((P, NT, P)),
                                                op0=ALU.mult, op1=ALU.add))
                    link(v.tensor_reduce(top, pb, AX, ALU.max))
                v.tensor_scalar(less_top(u), top, -1.0, None, ALU.mult).then_inc(scores_max, 1)
                if u >= 3 and u % 2 == 1:
                    keep_output(u // 2 - 1)
            keep_output(len(ATT_UNITS) // 2 - 1)

            dve.wait_ge(stats_turned, 1)
            row4 = slice(0, HG)
            top4 = top_row[row4]
            link(v.tensor_copy(top4, ps[row4, 0]))
            for gi in range(1, NG):
                link(v.tensor_tensor(token_blocks(top4), token_blocks(top4), unsort(ps[row4, gi]), ALU.max))
            for gi in range(NG):
                f = (lambda a: a) if gi == 0 else token_blocks
                last = v.tensor_tensor(f(weights[row4, gi]), by_group(gi, ps[row4, gi]), f(top4), ALU.subtract)
            last.then_inc(mix_max, 1)
            dve.wait_ge(mix_exp, 1)
            link(v.tensor_tensor(den[row4, 0], weights[row4, 0], ps[row4, NG], ALU.mult))
            for gi in range(1, NG):
                link(v.tensor_tensor(token_blocks(den[row4, 1]), token_blocks(weights[row4, gi]), unsort(ps[row4, NG + gi]), ALU.mult))
                link(v.tensor_tensor(den[row4, 0], den[row4, 0], den[row4, 1], ALU.add))
            v.reciprocal(den[row4, 1], den[row4, 0]).then_inc(mix_den, 1)
            for j in range(2):
                dve.wait_ge(spread, 1 if j == 0 else 2)
                term = top_row[:]
                link(v.tensor_tensor(y_c[:, j], o_win[:, j], ps[:, NG * j], ALU.mult))
                for gi in range(1, NG):
                    link(v.tensor_tensor(term, o_dil[:, gi - 1, j], ps[:, NG * j + gi], ALU.mult))
                    link(v.tensor_tensor(y_c[:, j], y_c[:, j], term, ALU.add))
                if j == 0:
                    dve.wait_ge(spread, 2)
                last = v.tensor_tensor(y_c[:, j], y_c[:, j], ps[:, 6 + j], ALU.mult)
            last.then_inc(y_c_ready, 1)
            dve.wait_ge(y_c_ready, 1)

            def y_part(t):
                return y_a[:, t] if t < NJ else cols(CONV_T + t - NJ)[:, 0] if t < 2 * NJ else y_c[:, t - 2 * NJ]

            for i, t in enumerate(PART_ORDER):
                dve.wait_ge(y_hi_ready, i + 1)
                v.tensor_tensor(y_lo[:, t], y_part(t), y_hi[:, t].bitcast(F), ALU.subtract).then_inc(y_lo_ready, 1)
            dve.wait_ge(g_att_ready, 1)
            for k in range(KT):
                if k < KT - 1:
                    dve.wait_ge(att_tile_done, k + 1)
                else:
                    dve.wait_ge(slot_used, S_ATT + 1)
                v.tensor_tensor(merged[:, k], ps[:, k], g_att[:, k], ALU.mult).then_inc(att_merged, 1)
            dve.wait_ge(att_merged, KT)
            for g in range(N_MERGE):
                dve.wait_ge(slot_used, S_MERGE + g + 1)
                dve.wait_ge(g_ab_ready, g + 1)
                pair = merged[:, 2 * g:2 * g + 2]
                for br in range(2):
                    b0 = 4 * (g % 2) + 2 * br
                    link(v.tensor_tensor(tmp[:], ps[:, b0:b0 + 2], g_ab[:, g % 2, br], ALU.mult))
                    last = v.tensor_tensor(pair, pair, tmp[:], ALU.add)
                    if br == 0:
                        link(last)
                last.then_inc(pair_merged, 1)
                dve.wait_ge(merged_ready, g + 1)
                v.tensor_tensor(a_lo[:, 2 * g:2 * g + 2], pair, a_hi[:, 2 * g:2 * g + 2].bitcast(F), ALU.subtract).then_inc(a_lo_ready, 1)

            dve.wait_ge(gains_loaded, 16)
            dve.wait_ge(xin_loaded, 16)
            normed(1, C_FPRE, h2_f32, KT, lambda i: add_normed(i, 0, x_in, gain_mix, x1, x1_ready) if i < NT else None)

            def ffn_in(i):
                for b in range(2):
                    n = i * 2 + b
                    bank = (S_FIN + b) % 2 * 2
                    dve.wait_ge(silu_sig, n + 1)
                    link(v.tensor_tensor(f_act[:], f_sig[:], ps[:, bank], ALU.mult))
                    v.tensor_tensor(f_act[:], f_act[:], ps[:, bank + 1], ALU.mult).then_inc(f_act_ready, 1)
                    dve.wait_ge(f_hi_ready, n + 1)
                    lo_ = f_lo[:].rearrange("p (n two) t -> p n two t", two=2)
                    hi_ = f_hi[:].rearrange("p (n two) t -> p n two t", two=2)
                    v.tensor_tensor(lo_[:, i, b], f_act[:], hi_[:, i, b].bitcast(F), ALU.subtract).then_inc(f_lo_ready, 1)
                    dve.wait_ge(f_lo_ready, n + 1)

            dve.wait_ge(a_lo_ready, NT + N_MERGE + NT)
            ch.loop(2)
            with dve.Fori(0, N_FIN // 2, 1) as i:
                ch.begin(i)
                ffn_in(i)
            ch.end(N_FIN // 2)
            dve.wait_ge(gain_ffn_loaded, 16)
            for t in range(NT):
                add_normed(t, 1, x1, gain_ffn, x1, row_ready)

        @block.tensor
        def _(pe):
            t_ = nc.tensor

            def three(dst, w0, w1, a0, a1, first, last):
                t_.matmul(dst, w0, a0, start=first, stop=False)
                t_.matmul(dst, w0, a1, start=False, stop=False)
                return t_.matmul(dst, w1, a0, start=False, stop=last)

            def by_channel(b, bank, ahi, alo, col_tiles=2):
                wh = w_hi[:, b].rearrange("p (k c) -> p k c", k=KT)
                wl = w_lo[:, b].rearrange("p (k c) -> p k c", k=KT)
                for m in range(col_tiles):
                    c = slice(m * P, (m + 1) * P)
                    for k in range(KT):
                        last = three(ps[:, bank + m], wh[:, k, c], wl[:, k, c], ahi[:, k], alo[:, k], k == 0, k == KT - 1)
                return last

            def by_token(b, ahi, alo, first, final, order=range(NT), before=lambda t: None):
                wh = w_hi[:, b].rearrange("p (k c) -> p k c", k=2)
                wl = w_lo[:, b].rearrange("p (k c) -> p k c", k=2)
                for t in order:
                    before(t)
                    s_ = slice(t * P, (t + 1) * P)
                    for k in range(2):
                        for half in range(2):
                            c = slice(half * SEQ, (half + 1) * SEQ)
                            last = three(ps[:, 2 * t + half], ahi(k)[:, s_], alo(k)[:, s_], wh[:, k, c], wl[:, k, c],
                                         first and k == 0, final and k == 1)
                    if final and t < NT - 1:
                        last.then_inc(z_tile_done, 1)
                return last

            pe.wait_ge(consts_ready, 1)
            pe.wait_ge(rows_loaded, 16 * 9)
            t_.transpose(ps[:, 7, 0:N_ROWS], param_rows[0:N_ROWS, :], ident[0:N_ROWS, 0:N_ROWS]).then_inc(rows_turned, 1)

            def turn_rows(src, turn):
                for t in range(NT):
                    pe.wait_ge(h_ready, turn * NT + t + 1)
                    for k in range(KT):
                        last = t_.transpose(ps[:, 2 * t + k // 4, k % 4 * P:(k % 4 + 1) * P], src[:, t, k * P:(k + 1) * P], ident[:])
                    last.then_inc(turned, 1)

            pe.wait_ge(params_ready, 1)
            turn_rows(x_tok, 0)
            pe.wait_ge(scaled, NT)
            pe.wait_ge(a_lo_ready, NT)

            def proj_pair(i):
                for b in range(2):
                    n = i * 2 + b
                    pe.wait_ge(lo_ready, n + 1)
                    if not isinstance(i, int):
                        pe.wait_ge(proj_out, n - 1)
                    by_channel(b, 2 * b, a_hi, a_lo).then_inc(slot_used, 1)

            passes(pe, proj_pair, N_RWKV // 2)
            n = N_RWKV - 1
            pe.wait_ge(lo_ready, n + 1)
            pe.wait_ge(proj_out, n - 1)
            by_channel(n % 2, 2 * (n % 2), a_hi, a_lo).then_inc(slot_used, 1)
            pe.wait_ge(proj_out, N_RWKV)

            pe.wait_ge(ups_loaded, 48)
            pe.wait_ge(state_zero, 1)

            def rwkv(T):
                def need(sig_, k=0):
                    pe.wait_ge(sig_.sem, sig_.at(T, k))

                def heads(t, h):
                    r = slice(HD * (h % 2), HD * (h % 2) + HD)
                    return t[r, h // 2]

                units = iter(range(2 * PER_T * KT))

                def fill(count):
                    for _ in range(count):
                        u = next(units)
                        q, kt = u // KT, u % KT
                        k, half = q // 2, q % 2
                        b = (N_RWKV + k) % 2
                        if u % (2 * KT) == 0:
                            pe.wait_ge(lo_ready, T * PER_T + (N_RWKV + k + 1))
                        if kt == 0 and not (isinstance(T, int) and q < 2):
                            pe.wait_ge(spill_copied, T * (2 * PER_T) + (q - 1))
                        wh = w_hi[:, b].rearrange("p (k c) -> p k c", k=KT)
                        wl = w_lo[:, b].rearrange("p (k c) -> p k c", k=KT)
                        c = slice(half * P, (half + 1) * P)
                        last = three(ps[:, 6 + half], wh[:, kt, c], wl[:, kt, c], a_hi[:, kt], a_lo[:, kt], kt == 0, kt == KT - 1)
                        if kt == KT - 1:
                            last.then_inc(slot_used if half else first_tile, 1)

                fill(12)
                need(lora_ready)
                for j in range(NJ):
                    c = slice(j * P, (j + 1) * P)
                    t_.matmul(ps[:, 0, c], lora_up[0:HD, c], xm[0:HD, RT - 2], start=True, stop=True)
                for j in range(NJ):
                    c = slice(j * P, (j + 1) * P)
                    last = t_.matmul(ps[:, 1, c], lora_up[HD:P, c], xm[HD:P, RT - 2], start=True, stop=True)
                last.then_inc(z_done.sem, 1)
                t_.matmul(ps[:, 2], xm[:, RT - 1], g_up[:], start=True, stop=True).then_inc(g_done.sem, 1)
                fill(2)
                need(sq_ready)
                t_.matmul(ps[:, 3], head_ones[:], sq[:].rearrange("p j t -> p (j t)"), start=True, stop=True).then_inc(ssq_done.sem, 1)
                fill(34)
                need(ops_ready)
                for dst, src in ((4, bd[:]), (5, kd[:]), (0, xm[:, 2 * NJ:3 * NJ])):
                    for j in range(NJ):
                        last = t_.transpose(ps[:, dst, j * P:(j + 1) * P], src[:, j], ident[:])
                last.then_inc(toks_done.sem, 1)
                for h in range(NH):
                    bank = 1 + h % 3
                    if h == 1:
                        need(g_ready)
                    if h >= 3:
                        need(mt_ready, h - 3)
                    rhs = heads(ar, h).rearrange("p a t -> p (a t)")
                    t_.matmul(ps[:, bank, 0:2 * P], heads(bd, h), rhs, start=True, stop=True)
                    t_.matmul(ps[:, bank, 2 * P:4 * P], heads(kd, h), rhs, start=True, stop=True).then_inc(mt_done.sem, 1)
                fill(2)
                need(toks_ready)
                for j in range(NJ):
                    last = t_.matmul(ps[:, 5, 2 * j:2 * j + 2], rk[:, j], head_ones[:, ::HD], start=True, stop=True)
                last.then_inc(bonus_done.sem, 1)
                need(mt_ready, NH - 1)
                for lv in range(LEVELS):
                    b = 1 << lv
                    if lv > 0:
                        need(t_ready, lv - 1)
                    for h in range(NH):
                        src = ident[:] if lv == 0 else tt[:, h]
                        rhs = src.rearrange("p (n two b) -> p n two b", two=2, b=b)[:, :, 0]
                        last = t_.matmul(ps[:, 0, h * HD:(h + 1) * HD].rearrange("p (n b) -> p n b", b=b), mt[:, h, 0], rhs,
                                         start=True, stop=True)
                    last.then_inc(q_done.sem, 1)
                    if lv == 0:
                        fill(2)
                    else:
                        if lv > 1:
                            need(w_ready, lv - 2)
                        for h in range(NH):
                            last = t_.transpose(ps[:, 3 + h // 4, h % 4 * P:(h % 4 + 1) * P], tt[:, h], ident[:])
                        last.then_inc(w_done.sem, 1)
                        fill(1)
                        need(q_ready, lv)
                        need(w_ready, lv - 1)
                        for h in range(NH):
                            last = t_.matmul(ps[:, 1, h * HD:(h + 1) * HD], wt[:, h], qb[:, h], start=True, stop=True)
                        last.then_inc(t_done.sem, 1)
                        fill(2)
                need(t_ready, LEVELS - 1)
                need(w_ready, LEVELS - 2)
                for h in range(NH):
                    last = t_.transpose(ps[:, 3 + h // 4, h % 4 * P:(h % 4 + 1) * P], tt[:, h], ident[:])
                last.then_inc(w_done.sem, 1)
                fill(2)
                need(w_ready, LEVELS - 1)
                for c in range(2):
                    r = slice(HD * c, HD * c + HD)
                    if c > 0:
                        need(s_ready, c - 1)
                    elif not isinstance(T, int):
                        pe.wait_ge(s_ready.sem, T * 2)

                    def pair(dst, a):
                        for j in range(NJ):
                            t_.matmul(ps[r, dst, j * P:(j + 1) * P], ar[:, j, a, r], state[:, j].rearrange("p h v -> p (h v)"),
                                      start=(j == 0), stop=False, skip_group_check=True)

                    def each(dst, lhs, rhs, end=False, rows=slice(0, P), hs=range(NH)):
                        for h in hs:
                            last = t_.matmul(ps[r, dst, h * HD:(h + 1) * HD], lhs[rows, h, r], rhs[rows, h], start=False, stop=end,
                                             skip_group_check=True)
                        return last

                    pair(4, 0)
                    each(4, mt[:, :, 2], v_tok, True).then_inc(x_done.sem, 1)
                    pair(5, 1)
                    each(5, mt[:, :, 3], v_tok, hs=range(NH - 1))
                    need(x_ready, c)
                    each(5, mt[:, :, 3], v_tok, hs=range(NH - 1, NH))
                    for h in range(NH):
                        last = t_.matmul(ps[r, 1, h * HD:(h + 1) * HD], wt[r, h, r], xs[r, h],
                                         start=True, stop=True)
                    last.then_inc(u_done.sem, 1)
                    fill(1)
                    need(u_ready, c)
                    for j in range(NJ):
                        cj = slice(j * P, (j + 1) * P)
                        uj = us[r, 2 * j:2 * j + 2].rearrange("p h v -> p (h v)")
                        vj = v_tok[r, 2 * j:2 * j + 2].rearrange("p h v -> p (h v)")
                        t_.matmul(ps[:, 2, cj], b_tok[r, j], uj, start=True, stop=False)
                        last = t_.matmul(ps[:, 2, cj], k_tok[r, j], vj, start=False, stop=True)
                    last.then_inc(s_done.sem, 1)
                    last = each(5, mt[:, :, 1], us, True, r)
                    if c == 1:
                        last.then_inc(y_done.sem, 1)
                    fill(2)
                fill(21)
                need(y_ready)
                for j in range(NJ):
                    last = t_.transpose(ps[:, 0, j * P:(j + 1) * P], y1[:, 2 * j:2 * j + 2].rearrange("p h v -> p (h v)"), ident[:])
                last.then_inc(y_turned.sem, 1)

            passes(pe, rwkv, NT)

            pe.wait_ge(y_a_ready.sem, NT)

            def left(m, bank):
                pe.wait_ge(lo_ready, S_REST + m + 1)
                by_channel((S_REST + m) % 2, bank, a_hi, a_lo).then_inc(slot_used, 1)

            for m in range(N_LEFT - 1):
                left(m, 2 * (m % 2))

            pe.wait_ge(qkv_loaded, 16)
            pe.wait_ge(spill_copied, 2 * (N_WIN - N_RWKV - 1))
            for t in range(AJ):
                vt = cols(ATT_T + 2 * AJ + t)[:, 0]
                for blk in range(NT):
                    src = vt[:, blk * P:(blk + 1) * P] if t < 2 else sort_tokens(vt)[:, blk]
                    last = t_.transpose(ps[:, t, blk * P:(blk + 1) * P], src, ident[:])
                last.then_inc(v_turned, 1)
            pe.wait_ge(sorted_ready, 8)
            pe.wait_ge(v_ready, AJ)

            def scores(u):
                gi, hh = ATT_UNITS[u]
                q, k = q_row(gi, hh, 0), q_row(gi, hh, 1)
                for n in range(NT):
                    if gi == 0:
                        k0 = max(0, n - 1)
                        dst = ps[:, 2 * (u % 2) + n // 2, (n % 2) * 2 * P + (P if n == 0 else 0):(n % 2 + 1) * 2 * P]
                    else:
                        k0 = n
                        dst = ps[:, 2 * (u % 2), n * P:(n + 1) * P]
                    last = t_.matmul(dst, q[:, n * P:(n + 1) * P], k[:, k0 * P:(n + 1) * P], start=True, stop=True)
                last.then_inc(scores_done, 1)

            def outputs(u):
                gi, hh = ATT_UNITS[u]
                pe.wait_ge(probs_t_ready, u + 1)
                if u >= 4:
                    pe.wait_ge(o_ready, u // 2 - 1)
                rows = slice(HD * (hh % 2), HD * (hh % 2) + HD)
                bl = blocks(gi)
                for i, (n, k) in enumerate(bl):
                    vt = cols(ATT_T + 2 * AJ + 2 * gi + hh // 2)[:, 0, k * P + HD * (hh % 2):k * P + HD * (hh % 2) + HD]
                    last = t_.matmul(ps[rows, 6 + u // 2 % 2, n * P:(n + 1) * P], vt, pt_buf[:, u % 2, i * P:(i + 1) * P],
                                     start=(i == 0 or bl[i - 1][0] != n), stop=(k == n))
                last.then_inc(pv_done, 1)

            scores(0)
            scores(1)
            for u, (gi, hh) in enumerate(ATT_UNITS):
                pe.wait_ge(probs_ready, u + 1)
                if u >= 1 and (gi == 0 or ATT_UNITS[u - 1][0] == 0):
                    pe.wait_ge(probs_t_ready, u)
                elif u >= 2:
                    pe.wait_ge(probs_t_ready, u - 1)
                for i, (n, k) in enumerate(blocks(gi)):
                    c = slice(P * (n + k + 1), P * (n + k + 2)) if gi == 0 else slice(P * n, P * (n + 1))
                    bank = 4 + (i // 4 if gi == 0 else u % 2)
                    last = t_.transpose(ps[:, bank, i % 4 * P:(i % 4 + 1) * P], p_buf[:, u % 2, c], ident[:])
                last.then_inc(probs_turned, 1)
                if u + 2 < len(ATT_UNITS):
                    scores(u + 2)
                if u >= 1:
                    outputs(u - 1)
            outputs(len(ATT_UNITS) - 1)
            for gi in range(NG):
                for t in range(NT):
                    t_.transpose(ps[0:HG, gi, t * P:(t + 1) * P], top_of(gi, t), ident[:])
                    last = t_.transpose(ps[0:HG, NG + gi, t * P:(t + 1) * P], sum_of(gi, t), ident[:])
            last.then_inc(stats_turned, 1)
            pe.wait_ge(o_ready, len(ATT_UNITS) // 2)
            left(N_LEFT - 1, 6)
            def spread_rows(dst, rows, j):
                return t_.matmul(dst, head_rows[0:HG, j * P:(j + 1) * P], rows, start=True, stop=True)

            pe.wait_ge(dist_ready, 2)
            pe.wait_ge(mix_exp, 1)
            for gi in range(NG):
                last = spread_rows(ps[:, gi], weights[0:HG, gi], 0)
            last.then_inc(spread, 1)
            pe.wait_ge(mix_den, 1)
            pe.wait_ge(spill_copied, 2 * (N_WIN - N_RWKV))
            for gi in range(NG):
                spread_rows(ps[:, NG + gi], weights[0:HG, gi], 1)
            for j in range(2):
                last = spread_rows(ps[:, 6 + j], den[0:HG, 1], j)
            last.then_inc(spread, 1)

            pe.wait_ge(y_lo_ready, 2)
            pe.wait_ge(lo_ready, S_ATT + 1)
            b = S_ATT % 2
            wh = w_hi[:, b].rearrange("p (k c) -> p k c", k=2)
            wl = w_lo[:, b].rearrange("p (k c) -> p k c", k=2)
            for m in range(KT):
                c = slice(m * P, (m + 1) * P)
                for k in range(2):
                    last = three(ps[:, m], wh[:, k, c], wl[:, k, c], y_hi[:, 2 * NJ + k], y_lo[:, 2 * NJ + k], k == 0, k == 1)
                last.then_inc(att_tile_done if m < KT - 1 else slot_used, 1)
            pe.wait_ge(y_lo_ready, BT)
            for g in range(N_MERGE):
                b = (S_MERGE + g) % 2
                wh = w_hi[:, b].rearrange("p (k c) -> p k c", k=KT)
                wl = w_lo[:, b].rearrange("p (k c) -> p k c", k=KT)
                pe.wait_ge(lo_ready, S_MERGE + g + 1)
                if g >= 2:
                    pe.wait_ge(pair_merged, g - 1)
                else:
                    pe.wait_ge(att_merged, 4 * (g + 1))
                for br in range(2):
                    for m in range(2):
                        c = slice(m * P, (m + 1) * P)
                        for k in range(NJ):
                            kt = br * NJ + k
                            last = three(ps[:, 4 * (g % 2) + 2 * br + m], wh[:, kt, c], wl[:, kt, c], y_hi[:, kt], y_lo[:, kt],
                                         k == 0, k == NJ - 1)
                last.then_inc(slot_used, 1)

            pe.wait_ge(pair_merged, N_MERGE - 1)
            for m in range(N_OUT):
                pe.wait_ge(a_lo_ready, NT + m + 1)
                pe.wait_ge(lo_ready, S_OUT + m + 1)
                by_token((S_OUT + m) % 2, lambda k: a_hi[:, 2 * m + k], lambda k: a_lo[:, 2 * m + k],
                         m == 0, m == N_OUT - 1,
                         before=lambda t: pe.wait_ge(pair_merged, N_MERGE) if m == 0 and t == 2 else None).then_inc(slot_used, 1)

            turn_rows(h2_tok, 1)
            pe.wait_ge(scaled, 2 * NT)
            pe.wait_ge(a_lo_ready, NT + N_MERGE + NT)

            def ffn_in(i):
                for b in range(2):
                    n = i * 2 + b
                    pe.wait_ge(lo_ready, n + S_FIN + 1)
                    if not isinstance(i, int):
                        pe.wait_ge(f_act_ready, n - 1)
                    par = (S_FIN + b) % 2
                    by_channel(par, 2 * par, a_hi, a_lo).then_inc(slot_used, 1)

            passes(pe, ffn_in, N_FIN // 2)
            pe.wait_ge(f_act_ready, N_FIN - 1)
            last_pair = (S_FOUT - 1) % 2
            for m in range(N_FOUT):
                pe.wait_ge(f_lo_ready, 2 * m + 2)
                pe.wait_ge(lo_ready, S_FOUT + m + 1)
                by_token((S_FOUT + m) % 2, lambda k: f_hi[:, 2 * m + k], lambda k: f_lo[:, 2 * m + k],
                         m == 0, m == N_FOUT - 1, *([(2, 3, 1 - last_pair, last_pair),
                                                     lambda t: pe.wait_ge(f_act_ready, N_FIN) if t == last_pair else None] if m == 0 else [])).then_inc(slot_used, 1)


_INS = ["x", "norm_mix_pre", "norm_mix_post", "norm_ffn_pre", "norm_ffn_post", "w_in", "rwkv_mu", "rwkv_w0", "rwkv_w_up",
        "rwkv_a0", "rwkv_a_up", "rwkv_g_up", "rwkv_k_k", "rwkv_k_a", "rwkv_r_k", "rwkv_ln_w", "rwkv_ln_b", "conv_w",
        "w_branch", "w_out", "w_ffn_in", "w_ffn_out"]


def kernel(**inputs):
    import numpy as _np
    import concourse.bacc as _bacc
    from concourse.bass_utils import run_bass_kernel_spmd as _run

    nc = _bacc.Bacc("TRN2", target_bir_lowering=False, num_devices=1)
    arrays, args = {}, []
    for name in _INS:
        a = _np.ascontiguousarray(inputs[name])
        arrays[name] = a
        args.append(nc.dram_tensor(name, a.shape, mybir.dt.from_np(a.dtype), kind="ExternalInput").ap())
    shape = inputs["x"].shape
    args.append(nc.dram_tensor("out", shape, mybir.dt.float32, kind="ExternalOutput").ap())
    args.append(nc.dram_tensor("spill", ((inputs["w_in"].shape[2] - inputs["rwkv_mu"].shape[1]) // 128, 128, shape[1]), mybir.dt.float32, kind="Internal").ap())
    hybrid_layer(nc, *args)
    r = _run(nc, [arrays], core_ids=[0])
    return r.results[0]["out"]
```

```python
import math
from contextlib import ExitStack

import concourse.bass as bass
from concourse import mybir


def hybrid_layer(nc, x, norm_mix_pre, norm_mix_post, norm_ffn_pre, norm_ffn_post, w_in, rwkv_mu,
                 rwkv_w0, rwkv_w_up, rwkv_a0, rwkv_a_up, rwkv_g_up, rwkv_k_k, rwkv_k_a, rwkv_r_k,
                 rwkv_ln_w, rwkv_ln_b, conv_w, w_branch, w_out, w_ffn_in, w_ffn_out, out, spill):
    F = mybir.dt.float32
    R = mybir.dt.float32r
    I32 = mybir.dt.int32
    ALU = mybir.AluOpType
    ACT = mybir.ActivationFunctionType
    AX = mybir.AxisListType.X

    P = 128
    SEQ, D = x.shape[1], x.shape[2]
    NT = SEQ // P
    KT = D // P
    HD = 64
    NH = rwkv_r_k.shape[1]
    RW = NH * HD
    NJ = RW // P
    CW = conv_w.shape[2]
    CJ = CW // P
    HG, NG = 4, 3
    DILATION = (1, 4, 16)
    AJ = HG * NG * HD // P
    WINDOW = 128
    STRIDE = 4
    FT = w_ffn_out.shape[1] // P
    DFF = FT * P
    RT = rwkv_mu.shape[1] // P
    GATE0 = w_in.shape[2] - 3 * D
    PROJ_T = GATE0 // P
    CONV_T = 0
    ATT_T = RT + 3 * CJ
    SPILL_CONV, SPILL_ATT, SPILL_GATE = 0, 3 * CJ, PROJ_T - RT
    BT = 2 * NJ + 2
    NORM_EPS, GN_EPS = 1e-6, 64e-5
    DECAY = math.exp(-0.5)
    NEG = -3.0e38
    PAD = 2
    PITCH = SEQ + PAD
    LEVELS = 6

    SC = 256
    SLOT = KT * SC
    N_RWKV = RT * P // SC
    N_WIN = w_in.shape[2] // SC
    PER_T = 6
    S_REST = N_RWKV + NT * PER_T
    N_LEFT = N_WIN - S_REST
    N_MERGE, N_OUT, N_FIN, N_FOUT = D // SC, KT // 2, FT, FT // 2
    S_ATT = N_WIN
    S_MERGE = S_ATT + 1
    S_OUT = S_MERGE + N_MERGE
    S_FIN = S_OUT + N_OUT
    S_FOUT = S_FIN + N_FIN
    N_SLOTS = S_FOUT + N_FOUT

    C_MU = 0
    C_W0 = C_MU + RT
    C_A0 = C_W0 + NJ
    C_KK = C_A0 + NJ
    C_KA = C_KK + NJ
    C_RK = C_KA + NJ
    C_CONV = C_RK + NJ
    C_PRE = C_CONV + 3 * CJ
    C_FPRE = C_PRE + KT
    N_ROWS = C_FPRE + KT
    C_OMKA = 64
    S_X, S_Z, S_EPS = 0, 16, 60

    with ExitStack() as ctx:
        top = [(nc.sbuf_base + 63) // 64 * 64]

        def size(shape):
            return (4 * math.prod(shape[1:]) + 31) // 32 * 32

        def fixed(name, shape, dt=F):
            t = nc.alloc_sbuf_tensor_at(name, shape, dt, offset=top[0])
            top[0] += size(shape)
            return t

        w_raw = fixed("w_raw", [P, 2, SLOT])
        w_hi = fixed("w_hi", [P, 2, SLOT], R)
        w_lo = fixed("w_lo", [P, 2, SLOT], R)
        a_hi = fixed("a_hi", [P, KT, SEQ], R)
        a_lo = fixed("a_lo", [P, KT, SEQ], R)
        ident = fixed("ident", [P, P])
        causal_chunk = fixed("causal_chunk", [P, 4, HD])
        chunk_run = fixed("chunk_run", [P, SEQ])
        head_rows = nc.alloc_sbuf_tensor_at("head_rows", [P, 2 * P], F, offset=top[0])
        level_mask = fixed("level_mask", [P, LEVELS, HD])
        head_ones = fixed("head_ones", [P, P])
        lora_up = fixed("lora_up", [P, RW])
        g_up = fixed("g_up", [P, RW])
        params = fixed("params", [P, 68])
        stat = fixed("stat", [P, 64])
        small = fixed("small", [P, 128])
        ARENA = top[0]

        def arena(name, shape, offset, dt=F):
            assert ARENA + offset + size(shape) <= nc.sbuf_usable_end, (name, offset)
            return nc.alloc_sbuf_tensor_at(name, shape, dt, offset=ARENA + offset), offset + size(shape)

        def up32(n):
            return (n + 31) // 32 * 32

        x_tok, o = arena("x_tok", [P, NT, D], 0)
        h_f32, o = arena("h_f32", [P, KT, SEQ], o)
        sq_x, o = arena("sq_x", [P, D], o)
        proj, AT_YC = arena("proj", [P, PROJ_T, PITCH], 0)
        AT_S = up32(RT * PITCH * 4)
        AT_C = up32((RT + CJ) * PITCH * 4)
        AT_Q = up32(ATT_T * PITCH * 4)
        y_c, AT_TAIL = arena("y_c", [P, 2, SEQ], AT_YC)
        causal, _ = arena("causal", [P, 2, P], AT_Q)
        param_rows, _ = arena("param_rows", [64, P], AT_TAIL + 5 * 4 * SEQ + 4096)
        PITCH4 = 4 * PITCH
        qk_sorted, o = arena("qk_sorted", [P, 2, 4, SEQ], AT_C)
        assert o <= AT_Q
        bias_win, o = arena("bias_win", [P, HG, 2 * P], AT_TAIL)
        bias_dil, AT_ROWS = arena("bias_dil", [P, (NG - 1) * HG, P], o)
        dist_i, o = arena("dist_i", [P, 2 * P], AT_ROWS, I32)
        rem_i, o = arena("rem_i", [P, 2 * P], o, I32)
        dist_f, o = arena("dist_f", [P, 2 * P], o)
        late_f, o = arena("late_f", [P, 2 * P], o)
        mask_f, o = arena("mask_f", [P, 2 * P], o)
        weights, o = arena("weights", [P, NG, SEQ], AT_ROWS)
        top_row, o = arena("top_row", [P, SEQ], o)
        p_buf, o = arena("p_buf", [P, 2, 2 * SEQ], up32((CONV_T + CJ) * PITCH4))
        pt_buf, o = arena("pt_buf", [P, 2, 2 * SEQ - P], o)
        assert o <= 3 * CJ * PITCH4
        o_win, o = arena("o_win", [P, 2, SEQ], up32((ATT_T + 2) * PITCH4))
        den, o = arena("den", [P, 2, SEQ], o)
        assert o <= (ATT_T + AJ) * PITCH4
        o_dil, o = arena("o_dil", [P, NG - 1, 2, SEQ], up32((ATT_T + AJ + 2) * PITCH4))
        assert o <= (ATT_T + 2 * AJ) * PITCH4
        spill_buf, o = arena("spill_buf", [P, 2, 2, SEQ], AT_S)
        assert o <= AT_C
        mt, o = arena("mt", [P, NH, 4, HD], AT_C)
        mab, o = arena("mab", [P, NH, P], o)
        bk_tok, o = arena("bk_tok", [P, 2, NJ, P], o)
        assert o <= AT_Q
        xm, o = arena("xm", [P, RT, P], AT_Q)
        sig, e = arena("sig", [P, 2, NJ, P], o)
        wt, _ = arena("wt", [P, NH, P], o)
        cum, o = arena("cum", [P, NJ, P], e)
        tt, _ = arena("tt", [P, NH, P], e)
        prev, o = arena("prev", [P, NJ, P], o)
        ep, o = arena("ep", [P, NJ, P], o)
        kk, e = arena("kk", [P, NJ, P], o)
        qb, _ = arena("qb", [P, NH, HD], o)
        sq, o = arena("sq", [P, NJ, P], e)
        xs, _ = arena("xs", [P, NH, HD], e)
        k2, e = arena("k2", [P, NJ, P], o)
        ar, o = arena("ar", [P, NJ, 2 * P], e)
        bkd, o = arena("bkd", [P, NJ, 2 * P], o)
        uv, o = arena("uv", [P, 2, NH, HD], o)
        assert o <= AT_YC, (o, AT_YC)
        rk, o = arena("rk", [P, NJ, P], AT_TAIL)
        state, o = arena("state", [P, NJ, 2, HD], o)
        g_tok, o = arena("g_tok", [P, NH, HD], o)
        y1, o = arena("y1", [P, NH, HD], o)
        y2, o = arena("y2", [P, NH, HD], o)
        ln_wb, o = arena("ln_wb", [P, 2, RW], o + 4 * NJ * P)
        y_a, o = arena("y_a", [P, NJ, SEQ], o)
        y_hi, o = arena("y_hi", [P, BT, SEQ], AT_C, R)
        y_lo, o = arena("y_lo", [P, BT, SEQ], o, R)
        merged, o = arena("merged", [P, KT, SEQ], o)
        g_att, _ = arena("g_att", [P, KT, SEQ], up32((CONV_T + CJ) * PITCH4))
        g_ab, o = arena("g_ab", [P, 2, 2, 2, SEQ], o)
        tmp, o = arena("tmp", [P, 2, SEQ], o)
        x_in, o = arena("x_in", [P, NT, D], AT_C)
        gain_mix, o = arena("gain_mix", [P, D], o)
        f_hi, o = arena("f_hi", [P, FT, SEQ], 0, R)
        f_lo, o = arena("f_lo", [P, FT, SEQ], o, R)
        x1, o = arena("x1", [P, NT, D], o)
        gain_ffn, o = arena("gain_ffn", [P, D], o)
        f_sig, e = arena("f_sig", [P, SEQ], o)
        f_act, e = arena("f_act", [P, SEQ], e)
        squares, _ = arena("squares", [P, D], o)
        row, e = arena("row", [P, D], e)
        h2_tok, o = arena("h2_tok", [P, NT, D], 0)
        h2_f32, o = arena("h2_f32", [P, KT, SEQ], o)

        ps = ctx.enter_context(nc.psum_tensor("ps", [P, 8, SEQ], F))

        class Signal:

            def __init__(self, name, per=1):
                self.sem, self.per = ctx.enter_context(nc.semaphore(name)), per

            def at(self, turn=0, k=0):
                return turn * self.per + k + 1

        def sem(name):
            return ctx.enter_context(nc.semaphore(name))

        raw_loaded = [sem("raw_loaded_even"), sem("raw_loaded_odd")]
        hi_ready, lo_ready, slot_used = sem("hi_ready"), sem("lo_ready"), sem("slot_used")
        x_loaded, rows_loaded, ups_loaded = [sem("x_loaded_0"), sem("x_loaded_1")], sem("rows_loaded"), sem("ups_loaded")
        ln_loaded, spilled = sem("ln_loaded"), [sem("spilled_even"), sem("spilled_odd")]
        qkv_loaded, conv_loaded = sem("qkv_loaded"), sem("conv_loaded")
        first_tile, spill_copied, dist_ready = sem("first_tile"), sem("spill_copied"), sem("dist_ready")
        g_att_ready, g_ab_ready = sem("g_att_ready"), sem("g_ab_ready")
        g_att_loaded, g_ab_loaded = sem("g_att_loaded"), [sem("g_ab_even"), sem("g_ab_odd")]
        xin_loaded, gains_loaded, out_stored = sem("xin_loaded"), sem("gains_loaded"), sem("out_stored")
        gain_ffn_loaded = sem("gain_ffn_loaded")
        dve_chain, act_chain, pool_chain = sem("dve_chain"), sem("act_chain"), sem("pool_chain")
        ident_ready = sem("ident_ready")
        consts_ready, params_ready, rows_turned = sem("consts_ready"), sem("params_ready"), sem("rows_turned")
        eps_ready = sem("eps_ready")
        root_ready, rstd_ready, h_ready = sem("root_ready"), sem("rstd_ready"), sem("h_ready")
        turned, scaled, a_hi_ready, a_lo_ready = sem("turned"), sem("scaled"), sem("a_hi_ready"), sem("a_lo_ready")
        proj_out = sem("proj_out")
        v_turned, v_ready = sem("v_turned"), sem("v_ready")
        scores_done, scores_max, probs_ready = sem("scores_done"), sem("scores_max"), sem("probs_ready")
        probs_turned, probs_t_ready, pv_done = sem("probs_turned"), sem("probs_t_ready"), sem("pv_done")
        sorted_ready, o_ready, stats_turned = sem("sorted_ready"), sem("o_ready"), sem("stats_turned")
        mix_max, mix_exp, mix_den, spread = sem("mix_max"), sem("mix_exp"), sem("mix_den"), sem("spread")
        y_c_ready = sem("y_c_ready")
        xm_ready, lora_ready, z_done, g_done = Signal("xm_ready"), Signal("lora_ready"), Signal("z_done"), Signal("g_done")
        z_ready, sig_ready, sums_run, exps_ready = Signal("z_ready"), Signal("sig_ready"), Signal("sums_run"), Signal("exps_ready")
        kk_ready, sq_ready, ssq_done, ssq_ready = Signal("kk_ready"), Signal("sq_ready"), Signal("ssq_done"), Signal("ssq_ready")
        norm_ready, ops_ready, g_ready = Signal("norm_ready"), Signal("ops_ready"), Signal("g_ready")
        toks_done, toks_ready, bonus_done = Signal("toks_done"), Signal("toks_ready"), Signal("bonus_done")
        mt_done, mt_ready = Signal("mt_done", NH // 2), Signal("mt_ready", NH // 2)
        q_done, q_ready = Signal("q_done", LEVELS - 1), Signal("q_ready", LEVELS)
        t_done, t_ready = Signal("t_done", LEVELS - 1), Signal("t_ready", LEVELS)
        tt_turned = Signal("tt_turned", LEVELS - 1)
        w_done, w_ready = Signal("w_done"), Signal("w_ready")
        x_done, x_ready = Signal("x_done", 2), Signal("x_ready", 2)
        u_done, u_ready = Signal("u_done", 2), Signal("u_ready", 2)
        s_done, s_ready = Signal("s_done", 2), Signal("s_ready", 2)
        y_done = Signal("y_done", 2)
        y_mid, y_sq, y_var = Signal("y_mid"), Signal("y_sq"), Signal("y_var")
        y_std, y_ready, y_turned, y_a_ready = Signal("y_std"), Signal("y_ready"), Signal("y_turned"), Signal("y_a_ready")
        state_zero = sem("state_zero")
        y_hi_ready, y_lo_ready = sem("y_hi_ready"), sem("y_lo_ready")
        att_tile_done = sem("att_tile_done")
        att_merged, pair_merged, merged_ready = sem("att_merged"), sem("pair_merged"), sem("merged_ready")
        z_tile_done, z_root, x1_ready = sem("z_tile_done"), sem("z_root"), sem("x1_ready")
        silu_sig, f_act_ready, f_hi_ready, f_lo_ready = sem("silu_sig"), sem("f_act_ready"), sem("f_hi_ready"), sem("f_lo_ready")
        row_ready = sem("row_ready")

        SPILLED = [16 * sum(1 for n in range(N_RWKV, N_WIN) if (n - N_RWKV) % 2 == b) for b in range(2)]

        block = ctx.enter_context(nc.Block())

        def cols(j0, n=1, lo=PAD, width=SEQ):
            return proj[:, j0:j0 + n, lo:lo + width]

        def q_row(gi, hh, which):
            rows, j = slice(HD * (hh % 2), HD * (hh % 2) + HD), hh // 2
            if gi == 0:
                return proj[rows, ATT_T + which * AJ + j, PAD:PAD + SEQ]
            return qk_sorted[rows, which, 2 * (gi - 1) + j]

        def sort_tokens(ap):
            return ap.rearrange("p (i r) -> p r i", r=STRIDE)

        def unsort(ap):
            return ap.rearrange("p (r i) -> p i r", r=STRIDE)

        def by_group(gi, ap):
            return ap if gi == 0 else unsort(ap)

        def token_blocks(ap):
            return ap.rearrange("p (i r) -> p i r", r=STRIDE)

        def over(ap, shape):
            return ap.unsqueeze(2).broadcast_to(shape)

        MT_PAIRS = [(0, 2), (1, 3), (4, 6), (5, 7)]
        mt_bank = lambda h: (1, 2, 3, 1)[[h in pair for pair in MT_PAIRS].index(True)]
        own = [slice(HD * c, HD * c + HD) for c in range(2)]
        other = [own[1], own[0]]

        first_half = [lambda t, b=1 << l: t.rearrange("p h (n two b) -> p h n two b", two=2, b=b)[:, :, :, 0, :]
                      for l in range(LEVELS)]

        ATT_UNITS = [(gi, hh) for gi in range(NG) for hh in range(HG)]

        def blocks(gi):
            if gi == 0:
                return [(n, k) for n in range(NT) for k in range(max(0, n - 1), n + 1)]
            return [(r, r) for r in range(NT)]

        PART_ORDER = [*range(2 * NJ, BT), *range(2 * NJ)]

        top_of = lambda gi, t=slice(0, NT): small[:, 0:NG * NT * HG].rearrange("p (g t h) -> p g t h", g=NG, t=NT)[:, gi, t]
        sum_of = lambda gi, t=slice(0, NT): stat[:, 0:NG * NT * HG].rearrange("p (g t h) -> p g t h", g=NG, t=NT)[:, gi, t]
        less_top = lambda u: small[:, 48 + NT * (u % 2):48 + NT * (u % 2) + NT]

        class Chain:

            def __init__(self, eng, s):
                self.eng, self.sem, self.base, self.k, self.per, self.turn = eng, s, 0, 0, 0, 0

            def link(self, ins):
                self.k += 1
                ins.then_inc(self.sem, 1)
                self.eng.wait_ge(self.sem, self.turn * self.per + self.base + self.k)

            def loop(self, per):
                self.base, self.k, self.per = self.base + self.k, 0, per

            def begin(self, turn):
                self.turn, self.k = turn, 0

            def end(self, turns):
                assert self.k == self.per, (self.k, self.per)
                self.base, self.k, self.per, self.turn = self.base + self.per * turns, 0, 0, 0

        def passes(eng, body, count):
            body(0)
            if count > 1:
                with eng.Fori(1, count, 1) as i:
                    body(i)

        @block.sync
        def _(sp):
            wi = w_in[0].rearrange("(k p) (n c) -> n p k c", p=P, c=SC)
            wo = w_out[0].rearrange("(n k p) c -> n p k c", p=P, k=2)
            wb = w_branch[0].rearrange("(k p) c -> p k c", p=P)
            wf = w_ffn_in[0].rearrange("(k p) (half n c) -> half n p k c", p=P, c=P, half=2)
            wd = w_ffn_out[0].rearrange("(n k p) c -> n p k c", p=P, k=2)

            def load(n, parts):
                b = par(n)
                if not (isinstance(n, int) and n < 2):
                    sp.wait_ge(lo_ready, n - 1)
                for dst, src in parts:
                    sp.dma_start(dst, src).then_inc(raw_loaded[b], 16)

            def par(n):
                return par.b
            half8 = lambda b: w_raw[:, b].rearrange("p (k c) -> p k c", k=KT)
            half2 = lambda b: w_raw[:, b].rearrange("p (k c) -> p k c", k=2)

            sp.dma_start(x_tok[:, 0:2], x[0].rearrange("(t p) d -> p t d", p=P)[:, 0:2]).then_inc(x_loaded[0], 16)
            par.b = 0
            load(0, [(half8(0), wi[0])])
            sp.dma_start(x_tok[:, 2:4], x[0].rearrange("(t p) d -> p t d", p=P)[:, 2:4]).then_inc(x_loaded[1], 16)
            sp.wait_ge(rows_loaded, 16 * 9)
            par.b = 1
            load(1, [(half8(1), wi[1])])
            wi2 = w_in[0].rearrange("(k p) (n two c) -> n two p k c", p=P, c=SC, two=2)
            with sp.Fori(1, S_REST // 2 + 1, 1) as i:
                for b in range(2):
                    par.b = b
                    load(i * 2 + b, [(half8(b), wi2[i, b])])
            sd = spill.rearrange("t p s -> p t s")
            sp.wait_ge(xm_ready.sem, NT)
            for b in range(2):
                sp.wait_ge(spilled[b], 16 * (3 * CJ // 4))
            sp.dma_start(cols(CONV_T, 3 * CJ), sd[:, SPILL_CONV:SPILL_CONV + 3 * CJ]).then_inc(conv_loaded, 16)
            par.b = (S_REST + 1) % 2
            load(S_REST + 1, [(half8(par.b), wi[S_REST + 1])])
            sp.wait_ge(y_a_ready.sem, NT)
            for b in range(2):
                sp.wait_ge(spilled[b], 16 * (NT * PER_T // 2))
            sp.dma_start(cols(ATT_T, 3 * AJ), sd[:, SPILL_ATT:SPILL_ATT + 3 * AJ]).then_inc(qkv_loaded, 16)
            for n in range(S_REST + 2, N_WIN):
                par.b = n % 2
                load(n, [(half8(par.b), wi[n])])
            par.b = S_ATT % 2
            load(S_ATT, [(half2(par.b), wb[:, 2 * NJ:BT, :])])
            for g in range(N_MERGE):
                par.b = (S_MERGE + g) % 2
                load(S_MERGE + g, [(half8(par.b), wb[:, 0:2 * NJ, g * SC:(g + 1) * SC])])
                if g == 0:
                    for b in range(2):
                        sp.wait_ge(spilled[b], SPILLED[b])
                    sp.wait_ge(pv_done, len(ATT_UNITS))
                    gate = [sd[:, SPILL_GATE + br * KT:SPILL_GATE + (br + 1) * KT] for br in range(3)]
                    sp.dma_start(g_att[:], gate[2]).then_inc(g_att_loaded, 16)
                    sp.wait_ge(y_lo_ready, 2)
                if g >= 2:
                    sp.wait_ge(pair_merged, g - 1)
                for br in range(2):
                    sp.dma_start(g_ab[:, g % 2, br], gate[br][:, 2 * g:2 * g + 2]).then_inc(g_ab_loaded[g % 2], 16)
            for m in range(N_OUT):
                par.b = (S_OUT + m) % 2
                load(S_OUT + m, [(half2(par.b), wo[m])])
            sp.wait_ge(slot_used, S_OUT)
            sp.wait_ge(pair_merged, N_MERGE)
            sp.dma_start(x_in[:], x[0].rearrange("(t p) d -> p t d", p=P)).then_inc(xin_loaded, 16)
            sp.dma_start(gain_mix[:], norm_mix_post.broadcast_to((P, D))).then_inc(gains_loaded, 16)
            sp.dma_start(gain_ffn[:], norm_ffn_post.broadcast_to((P, D))).then_inc(gain_ffn_loaded, 16)
            wf2 = w_ffn_in[0].rearrange("(k p) (half n two c) -> n two half p k c", p=P, c=P, half=2, two=2)
            with sp.Fori(0, N_FIN // 2, 1) as i:
                for b in range(2):
                    par.b = (S_FIN + b) % 2
                    dst = w_raw[:, par.b].rearrange("p (k half c) -> p k half c", k=KT, half=2)
                    load(i * 2 + (S_FIN + b), [(dst[:, :, 0], wf2[i, b, 0]), (dst[:, :, 1], wf2[i, b, 1])])
            for m in range(N_FOUT):
                par.b = (S_FOUT + m) % 2
                load(S_FOUT + m, [(half2(par.b), wd[m])])
            sp.wait_ge(out_stored, 16 * NT)

        def raw_value(n, i=None, stride=2):
            extra = sum(1 for m in range(S_FIN, min(n + 1, S_FOUT)) if m % 2 == n % 2)
            value = 16 * (n // 2 + 1 + extra)
            if i is None:
                return value
            return i * (stride // 2 * (32 if n >= S_FIN else 16)) + value

        @block.gpsimd
        def _(pool):
            g = nc.gpsimd
            ch = Chain(pool, pool_chain)
            link = ch.link
            link(g.memset(ident[:], 0.0))
            g.affine_select(out=ident[:], in_=ident[:], compare_op=ALU.not_equal, fill=1.0, base=0,
                            pattern=[[-1, P]], channel_multiplier=1).then_inc(ident_ready, 1)
            pool.wait_ge(ident_ready, 1)
            link(g.memset(level_mask[:], 1.0))
            link(g.memset(causal[:], 1.0))
            link(g.memset(head_ones[:], 0.0))
            link(g.memset(chunk_run[:], 1.0))
            for half in range(2):
                rows = slice(HD * half, HD * half + HD)
                link(g.memset(head_ones[rows, rows], 1.0))
            link(g.memset(chunk_run[:].rearrange("p (n c) -> p n c", c=HD)[:, :, 0:1], 0.0))
            for inclusive in range(2):
                link(g.affine_select(out=causal[:, inclusive], in_=causal[:, inclusive], compare_op=ALU.is_gt,
                                fill=0.0, base=inclusive, pattern=[[1, P]], channel_multiplier=-1))
            for lv in range(LEVELS):
                b = 1 << lv
                nb = HD // b
                m = level_mask[:, lv].rearrange("p (n b) -> p n b", b=b)
                link(g.affine_select(out=m, in_=m, compare_op=ALU.is_ge, fill=0.0, base=-b,
                                pattern=[[-2 * b, nb], [0, b]], channel_multiplier=1))
            for lv in range(LEVELS):
                b = 1 << lv
                nb = HD // b
                m = level_mask[:, lv].rearrange("p (n b) -> p n b", b=b)
                link(g.affine_select(out=m, in_=m, compare_op=ALU.is_ge, fill=0.0, base=2 * b - 1,
                                pattern=[[2 * b, nb], [0, b]], channel_multiplier=-1))
            for half in range(2):
                r = slice(HD * half, HD * half + HD)
                link(g.tensor_copy(causal_chunk[r, 0::3], causal[r, 1:2, r].broadcast_to((HD, 2, HD))))
                last = g.tensor_copy(causal_chunk[r, 1:3], causal[r, 0:1, r].broadcast_to((HD, 2, HD)))
                if half == 0:
                    link(last)
            last.then_inc(consts_ready, 1)
            pool.wait_ge(consts_ready, 1)

            def low(n, b):
                pool.wait_ge(hi_ready, n + 1)
                g.tensor_tensor(w_lo[:, b], w_raw[:, b], w_hi[:, b].bitcast(F), ALU.subtract).then_inc(lo_ready, 1)

            with pool.Fori(0, S_REST // 2 + 1, 1) as i:
                for b in range(2):
                    low(i * 2 + b, b)
            pool.wait_ge(y_a_ready.sem, NT)
            g.iota(dist_i[:], [[-1, 2 * P]], base=P, channel_multiplier=1).then_inc(dist_ready, 1)
            link(g.memset(head_rows[:], 1.0))
            link(g.affine_select(out=head_rows[:], in_=head_rows[:], compare_op=ALU.is_ge, fill=0.0, base=0,
                                 pattern=[[1, 2 * P]], channel_multiplier=-HD))
            g.affine_select(out=head_rows[:], in_=head_rows[:], compare_op=ALU.is_ge, fill=0.0, base=HD - 1,
                                 pattern=[[-1, 2 * P]], channel_multiplier=HD).then_inc(dist_ready, 1)
            with pool.Fori(S_REST // 2 + 1, N_SLOTS // 2, 1) as i:
                for b in range(2):
                    low(i * 2 + b, b)

        @block.scalar
        def _(act):
            s = nc.scalar
            ch = Chain(act, act_chain)
            link = ch.link

            def high(n, loaded, b):
                act.wait_ge(raw_loaded[b], loaded)
                if not (isinstance(n, int) and n < 2):
                    act.wait_ge(slot_used, n - 1)
                s.copy(w_hi[:, b], w_raw[:, b]).then_inc(hi_ready, 1)

            def root_mean_square(src, junk, c, done):
                link(s.activation(junk, src, ACT.Square, accum_out=stat[:, c:c + 1]))
                s.activation(stat[:, c:c + 1], stat[:, c:c + 1], ACT.Sqrt, bias=stat[:, S_EPS:S_EPS + 1],
                             scale=1.0 / D).then_inc(done, 1)

            def z_root_of(t, turn, slots):
                if t < NT - 1:
                    act.wait_ge(z_tile_done, turn * (NT - 1) + t + 1)
                else:
                    act.wait_ge(slot_used, slots)
                root_mean_square(ps[:, 2 * t:2 * t + 2].rearrange("p a b -> p (a b)"), squares[:], S_Z + t, z_root)

            def normed(turn, src, dst, f32, junk, ready, ahead):
                lag = 1 if turn else 0
                for i in range(NT + 2):
                    ahead(i)
                    j = i - lag
                    if 0 <= j < NT:
                        ready(j)
                        root_mean_square(src[:, j], junk, S_X + j, root_ready)
                    if turn == 1 and 0 <= j < NT:
                        act.wait_ge(rstd_ready, j + 1)
                        s.activation(dst[:, j], src[:, j], ACT.Copy, scale=stat[:, S_X + j:S_X + j + 1]).then_inc(h_ready, 1)
                    if i >= 2:
                        c = slice((i - 2) * P, (i - 1) * P)
                        act.wait_ge(scaled, turn * NT + i - 1)
                        s.copy(a_hi[:, :, c], f32[:, :, c]).then_inc(a_hi_ready, 1)

            rows = [(rwkv_mu[0], RT, C_MU), (rwkv_w0[0], NJ, C_W0), (rwkv_a0[0], NJ, C_A0), (rwkv_k_k[0], NJ, C_KK),
                    (rwkv_k_a[0], NJ, C_KA), (norm_mix_pre[0], KT, C_PRE), (norm_ffn_pre[0], KT, C_FPRE)]
            for src, n, c in rows:
                act.dma_start(param_rows[c:c + n, :], src.rearrange("(a b) -> a b", b=P)).then_inc(rows_loaded, 16)
            act.dma_start(param_rows[C_RK:C_RK + NJ, :], rwkv_r_k[0].rearrange("(a b) c -> a (b c)", b=2)).then_inc(rows_loaded, 16)
            act.dma_start(param_rows[C_CONV:C_CONV + 3 * CJ, :],
                          conv_w[0].rearrange("k (a b) -> (k a) b", b=P)).then_inc(rows_loaded, 16)

            act.wait_ge(eps_ready, 1)
            normed(0, x_tok, x_tok, h_f32, sq_x[:], lambda j: act.wait_ge(x_loaded[j // 2], 16),
                   lambda i: high(0, raw_value(0), 0) if i == 2 else None)
            high(1, raw_value(1), 1)
            act.dma_start(lora_up[0:HD, :], rwkv_w_up[0]).then_inc(ups_loaded, 16)
            act.dma_start(lora_up[HD:P, :], rwkv_a_up[0]).then_inc(ups_loaded, 16)
            act.dma_start(g_up[:], rwkv_g_up[0]).then_inc(ups_loaded, 16)
            act.wait_ge(params_ready, 1)
            act.dma_start(ln_wb[:, 0], rwkv_ln_w.broadcast_to((P, RW))).then_inc(ln_loaded, 16)
            act.dma_start(ln_wb[:, 1], rwkv_ln_b.broadcast_to((P, RW))).then_inc(ln_loaded, 16)
            for n in range(2, N_RWKV + 2):
                high(n, raw_value(n), n % 2)

            beside = spill[0:2 * NT * PER_T].rearrange("(i k two) p s -> i k p two s", k=PER_T, two=2)

            def rwkv(T):
                def need(sig_, k=0):
                    act.wait_ge(sig_.sem, sig_.at(T, k))

                def evacuate(q):
                    k, half = q // 2, q % 2
                    b = k % 2
                    if half == 0:
                        act.wait_ge(first_tile, T * PER_T + (k + 1))
                        if not (isinstance(T, int) and k < 2):
                            act.wait_ge(spilled[b], T * (8 * PER_T) + 16 * (k // 2))
                    else:
                        act.wait_ge(slot_used, T * PER_T + (N_RWKV + k + 1))
                    s.copy(spill_buf[:, b, half], ps[:, 6 + half]).then_inc(spill_copied, 1)
                    if half == 1:
                        act.wait_ge(spill_copied, T * (2 * PER_T) + (q + 1))
                        act.dma_start(beside[T, k], spill_buf[:, b]).then_inc(spilled[b], 16)
                        n = N_RWKV + k + 2
                        high(T * PER_T + n, raw_value(n, T, PER_T), n % 2)

                need(xm_ready)
                s.activation(xm[0:HD, RT - 2], xm[0:HD, RT - 2], ACT.Tanh)
                s.activation(xm[:, RT - 1], xm[:, RT - 1], ACT.Sigmoid).then_inc(lora_ready.sem, 1)
                need(kk_ready)
                s.activation(sq[:], kk[:], ACT.Square).then_inc(sq_ready.sem, 1)
                evacuate(0)
                need(z_ready)
                s.activation(sig[:], sig[:], ACT.Sigmoid).then_inc(sig_ready.sem, 1)
                need(g_done)
                s.copy(g_tok[:], ps[:, 2].rearrange("p (h c) -> p h c", h=NH)).then_inc(g_ready.sem, 1)
                evacuate(1)
                need(sums_run)
                s.activation(ep[:], cum[:], ACT.Exp, scale=-DECAY)
                s.activation(prev[:], prev[:], ACT.Exp, scale=-DECAY)
                s.activation(cum[:], cum[:], ACT.Exp, scale=DECAY).then_inc(exps_ready.sem, 1)
                evacuate(2)
                need(ssq_ready)
                s.activation(sq[:], sq[:], ACT.Sqrt).then_inc(norm_ready.sem, 1)
                for q in (3, 4):
                    evacuate(q)
                need(toks_done)
                for c in range(2):
                    s.copy(bk_tok[:, c], ps[:, 4 + c].rearrange("p (h c) -> p h c", h=NJ))
                for c in range(2):
                    last = s.copy(uv[own[c], c], ps[own[c], 0].rearrange("p (h c) -> p h c", h=NH))
                last.then_inc(toks_ready.sem, 1)
                evacuate(5)
                evacuate(6)
                evacuate(7)
                need(w_done)
                s.copy(wt[:], ps[:, 3:5].rearrange("p a (h t) -> p (a h) t", t=P)).then_inc(w_ready.sem, 1)
                for c in range(2):
                    r = other[c]
                    need(x_done, c)
                    s.copy(xs[r], ps[r, 4 + c].rearrange("p (h v) -> p h v", h=NH)).then_inc(x_ready.sem, 1)
                    need(u_done, c)
                    s.copy(uv[r, c], ps[r, 1].rearrange("p (h v) -> p h v", h=NH)).then_inc(u_ready.sem, 1)
                    if c == 0:
                        evacuate(8)
                need(y_mid)
                s.activation(y2[:], y1[:], ACT.Square).then_inc(y_sq.sem, 1)
                evacuate(9)
                need(y_var)
                s.activation(small[:, 48:48 + NH], small[:, 48:48 + NH], ACT.Sqrt).then_inc(y_std.sem, 1)
                evacuate(10)
                evacuate(11)
                need(y_turned)
                dst = y_a[:].rearrange("p j (t c) -> p j t c", c=P)
                s.copy(dst[:, :, T], ps[:, 0].rearrange("p (j c) -> p j c", j=NJ)).then_inc(y_a_ready.sem, 1)

            act.wait_ge(state_zero, 1)
            passes(act, rwkv, NT)

            left = spill[2 * NT * PER_T:].rearrange("(n two) p s -> n p two s", two=2)

            def keep(m, bank):
                n, b = S_REST + m, (S_REST - N_RWKV + m) % 2
                act.wait_ge(slot_used, n + 1)
                act.wait_ge(spilled[b], 16 * ((n - N_RWKV) // 2))
                s.copy(spill_buf[:, b], ps[:, bank:bank + 2]).then_inc(spill_copied, 2)
                act.wait_ge(spill_copied, 2 * (n - N_RWKV) + 2)
                act.dma_start(left[m], spill_buf[:, b]).then_inc(spilled[b], 16)
                high(n + 2, raw_value(n + 2), n % 2)

            for m in range(N_LEFT - 1):
                keep(m, 2 * ((m + 1) % 2))
            def sort_heads(which):
                if which == 0:
                    act.wait_ge(qkv_loaded, 16)
                for j in range(4):
                    s.copy(qk_sorted[:, which, j].rearrange("p (r i) -> p r i", r=STRIDE),
                           sort_tokens(cols(ATT_T + which * AJ + 2 + j)[:, 0])).then_inc(sorted_ready, 1)

            n_units = len(ATT_UNITS)
            for u in range(n_units + 1):
                if u < n_units:
                    gi, hh = ATT_UNITS[u]
                    act.wait_ge(scores_max, u + 1)
                    for t in range(NT):
                        if gi == 0:
                            c = slice(2 * P * t + (P if t == 0 else 0), 2 * P * (t + 1))
                        else:
                            c = slice(P * t, P * (t + 1))
                        last = s.activation(p_buf[:, u % 2, c], p_buf[:, u % 2, c], ACT.Exp, bias=less_top(u)[:, t:t + 1],
                                            accum_out=sum_of(gi, t)[:, hh:hh + 1])
                    last.then_inc(probs_ready, 1)
                if u < 2:
                    sort_heads(u)
                if u > 0:
                    w = u - 1
                    act.wait_ge(probs_turned, w + 1)
                    if w >= 2:
                        act.wait_ge(pv_done, w - 1)
                    if ATT_UNITS[w][0] == 0:
                        s.copy(pt_buf[:, w % 2], ps[:, 4:6].rearrange("p a b -> p (a b)")[:, 0:2 * SEQ - P]).then_inc(probs_t_ready, 1)
                    else:
                        s.copy(pt_buf[:, w % 2, 0:SEQ], ps[:, 4 + w % 2]).then_inc(probs_t_ready, 1)
            act.wait_ge(mix_max, 1)
            s.activation(weights[0:HG], weights[0:HG], ACT.Exp).then_inc(mix_exp, 1)
            keep(N_LEFT - 1, 6)

            def y_part(t):
                return y_a[:, t] if t < NJ else cols(CONV_T + t - NJ)[:, 0] if t < 2 * NJ else y_c[:, t - 2 * NJ]

            act.wait_ge(y_a_ready.sem, NT)
            for t in PART_ORDER:
                if t >= 2 * NJ:
                    act.wait_ge(y_c_ready, t - 2 * NJ + 1)
                s.copy(y_hi[:, t], y_part(t)).then_inc(y_hi_ready, 1)
            def gates(g):
                act.wait_ge(g_ab_loaded[g % 2], 32 * (g // 2 + 1))
                s.activation(g_ab[:, g % 2], g_ab[:, g % 2], ACT.Sigmoid).then_inc(g_ab_ready, 1)

            act.wait_ge(g_att_loaded, 16)
            s.activation(g_att[:], g_att[:], ACT.Sigmoid).then_inc(g_att_ready, 1)
            gates(0)
            high(S_ATT + 2, raw_value(S_ATT + 2), (S_ATT + 2) % 2)
            gates(1)
            for g in range(N_MERGE):
                high(S_MERGE + g + 2, raw_value(S_MERGE + g + 2), (S_MERGE + g) % 2)
                act.wait_ge(pair_merged, g + 1)
                s.copy(a_hi[:, 2 * g:2 * g + 2], merged[:, 2 * g:2 * g + 2]).then_inc(merged_ready, 1)
                if g + 2 < N_MERGE:
                    gates(g + 2)

            for m in range(N_OUT - 2):
                high(S_OUT + m + 2, raw_value(S_OUT + m + 2), (S_OUT + m) % 2)

            def before_norm(i):
                if i < NT:
                    z_root_of(i, 0, S_FIN)
                elif i == NT:
                    high(S_FIN, raw_value(S_FIN), S_FIN % 2)

            normed(1, x1, h2_tok, h2_f32, squares[:], lambda j: act.wait_ge(x1_ready, j + 1), before_norm)
            high(S_FIN + 1, raw_value(S_FIN + 1), (S_FIN + 1) % 2)

            def ffn_in(i):
                for b in range(2):
                    n = i * 2 + b
                    act.wait_ge(slot_used, n + S_FIN + 1)
                    s.activation(f_sig[:], ps[:, (S_FIN + b) % 2 * 2], ACT.Sigmoid).then_inc(silu_sig, 1)
                    high(n + S_FIN + 2, raw_value(S_FIN + 2 + b, i) if not isinstance(i, int) else raw_value(S_FIN + 2 + b + 2 * i),
                         (S_FIN + b) % 2)
                    act.wait_ge(f_act_ready, n + 1)
                    dst = f_hi[:].rearrange("p (n two) t -> p n two t", two=2)
                    s.copy(dst[:, i, b], f_act[:]).then_inc(f_hi_ready, 1)

            with act.Fori(0, N_FIN // 2 - 1, 1) as i:
                ffn_in(i)
            ffn_in(N_FIN // 2 - 1)
            for m in range(N_FOUT - 2):
                high(S_FOUT + m + 2, raw_value(S_FOUT + m + 2), (S_FOUT + m) % 2)
            for t in range(NT + 1):
                if t < NT:
                    z_root_of(t, 1, N_SLOTS)
                if t > 0:
                    act.wait_ge(row_ready, t)
                    act.dma_start(out[0].rearrange("(t p) d -> t p d", p=P)[t - 1], x1[:, t - 1]).then_inc(out_stored, 16)

        @block.vector
        def _(dve):
            v = nc.vector
            ch = Chain(dve, dve_chain)
            link = ch.link

            def recip_root(root, value, c, done=None):
                dve.wait_ge(root, value)
                last = v.reciprocal(stat[:, c:c + 1], stat[:, c:c + 1])
                link(last) if done is None else last.then_inc(done, 1)

            def add_normed(t, turn, xin, gain, dst, done):
                recip_root(z_root, turn * NT + t + 1, S_Z + t)
                link(v.scalar_tensor_tensor(out=row[:], in0=ps[:, 2 * t:2 * t + 2].rearrange("p a b -> p (a b)"),
                                            scalar=stat[:, S_Z + t:S_Z + t + 1], in1=gain[:], op0=ALU.mult, op1=ALU.mult))
                v.tensor_tensor(dst[:, t], xin[:, t], row[:], ALU.add).then_inc(done, 1)
                dve.wait_ge(done, t + 1)

            def normed(turn, c_gain, f32, base, ahead):
                lag = 1 if turn else 0

                def gained(t):
                    dve.wait_ge(turned, turn * NT + t + 1)
                    v.tensor_tensor(f32[:, :, t * P:(t + 1) * P],
                                    ps[:, 2 * t:2 * t + 2].rearrange("p a (b c) -> p (a b) c", c=P),
                                    over(params[:, c_gain:c_gain + KT], (P, KT, P)), ALU.mult).then_inc(scaled, 1)

                def low_part(t):
                    if t >= 0:
                        c = slice(t * P, (t + 1) * P)
                        dve.wait_ge(a_hi_ready, turn * NT + t + 1)
                        v.tensor_tensor(a_lo[:, :, c], f32[:, :, c], a_hi[:, :, c].bitcast(F), ALU.subtract).then_inc(a_lo_ready, 1)

                for i in range(NT + 2):
                    j = i - lag
                    if 0 <= j < NT and turn == 0:
                        recip_root(root_ready, j + 1, S_X + j)
                        v.tensor_scalar(x_tok[:, j], x_tok[:, j], stat[:, S_X + j:S_X + j + 1], None, ALU.mult).then_inc(h_ready, 1)
                    elif 0 <= j < NT:
                        recip_root(root_ready, NT + j + 1, S_X + j, rstd_ready)
                    ahead(i)
                    if lag:
                        low_part(i - 2)
                    if 1 <= i <= NT:
                        gained(i - 1)
                    if not lag:
                        low_part(i - 2)

            v.memset(stat[:, S_EPS:S_EPS + 1], NORM_EPS).then_inc(eps_ready, 1)
            dve.wait_ge(rows_turned, 1)
            link(v.tensor_copy(params[:, 0:N_ROWS], ps[:, 7, 0:N_ROWS]))
            v.tensor_scalar(params[:, C_OMKA:C_OMKA + NJ], params[:, C_KA:C_KA + NJ], -1.0, 1.0, ALU.mult, ALU.add).then_inc(params_ready, 1)
            normed(0, C_PRE, h_f32, 0, lambda i: None)
            dve.wait_ge(a_lo_ready, NT)
            link(v.memset(proj[:, 0:RT, 0:PAD], 0.0))

            for n in range(N_RWKV):
                dve.wait_ge(slot_used, n + 1)
                v.tensor_copy(cols(2 * n, 2), ps[:, 2 * (n % 2):2 * (n % 2) + 2]).then_inc(proj_out, 1)
            dve.wait_ge(proj_out, N_RWKV)

            dve.wait_ge(consts_ready, 1)
            link(v.memset(mab[:], 0.0))
            v.memset(state[:], 0.0).then_inc(state_zero, 1)
            dve.wait_ge(state_zero, 1)
            dve.wait_ge(ln_loaded, 32)

            def rwkv(T):
                def need(sig_, k=0):
                    dve.wait_ge(sig_.sem, sig_.at(T, k))

                r_, k_, v_ = xm[:, 0:NJ], xm[:, NJ:2 * NJ], xm[:, 2 * NJ:3 * NJ]
                four = (P, NJ, P)

                def par(c, n=NJ):
                    return over(params[:, c:c + n], (P, n, P))

                now = proj[:, 0:RT, PAD:PITCH].rearrange("p j (t c) -> p j t c", c=P)[:, :, T]
                before = proj[:, 0:RT, PAD - 1:PITCH - 1].rearrange("p j (t c) -> p j t c", c=P)[:, :, T]
                link(v.tensor_tensor(xm[:], before, now, ALU.subtract))
                link(v.tensor_tensor(xm[:], xm[:], par(C_MU, RT), ALU.mult))
                v.tensor_tensor(xm[:], xm[:], now, ALU.add).then_inc(xm_ready.sem, 1)
                need(xm_ready)
                v.tensor_tensor(kk[:], k_, par(C_KK), ALU.mult).then_inc(kk_ready.sem, 1)
                need(z_done)
                v.tensor_tensor(sig[:, 0], ps[:, 0].rearrange("p (j t) -> p j t", j=NJ), par(C_W0), ALU.add)
                v.tensor_tensor(sig[:, 1], ps[:, 1].rearrange("p (j t) -> p j t", j=NJ), par(C_A0), ALU.add).then_inc(z_ready.sem, 1)
                need(ssq_done)
                need(sq_ready)
                v.tensor_scalar(sq[:], ps[:, 3].rearrange("p (j t) -> p j t", j=NJ), 1e-12, None, ALU.max).then_inc(ssq_ready.sem, 1)
                need(sig_ready)
                link(v.tensor_tensor_scan(cum[:].rearrange("p j t -> p (j t)"), chunk_run[:],
                                          sig[:, 0].rearrange("p j t -> p (j t)"), 0.0, ALU.mult, ALU.add))
                v.tensor_tensor(prev[:], cum[:], sig[:, 0], ALU.subtract).then_inc(sums_run.sem, 1)
                link(v.tensor_tensor(k2[:], sig[:, 1], par(C_KA), ALU.mult))
                link(v.tensor_tensor(k2[:], k2[:], par(C_OMKA), ALU.add))
                link(v.tensor_tensor(k2[:], k2[:], k_, ALU.mult))
                link(v.tensor_tensor(rk[:], r_, k2[:], ALU.mult))
                link(v.tensor_tensor(rk[:], rk[:], par(C_RK), ALU.mult))
                need(norm_ready)
                link(v.reciprocal(sq[:], sq[:]))
                link(v.tensor_tensor(kk[:], kk[:], sq[:], ALU.mult))
                link(v.tensor_tensor(sq[:], kk[:], sig[:, 1], ALU.mult))
                need(exps_ready)
                four_way = lambda t: t.rearrange("p j (x t) -> p j x t", t=HD)
                v.tensor_tensor(four_way(ar[:])[:, :, 0::3], four_way(r_), four_way(ep[:]), ALU.mult)
                v.tensor_tensor(four_way(bkd[:])[:, :, 0::3], four_way(k2[:]), four_way(cum[:]), ALU.mult)
                v.tensor_tensor(bkd[:, :, HD:HD + P], sq[:], cum[:], ALU.mult)
                ends = ep[:].rearrange("p j (c t) -> p c j t", t=HD)[:, :, :, HD - 1:HD]
                for c in range(2):
                    v.tensor_tensor(small[:, 64 + 8 * c:72 + 8 * c].rearrange("p (j h) -> p j h", h=2),
                                    ends[:, c].broadcast_to((P, NJ, 2)),
                                    head_ones[:, ::HD].unsqueeze(1).broadcast_to((P, NJ, 2)), ALU.mult)
                v.scalar_tensor_tensor(out=ar[:, :, HD:HD + P], in0=kk[:], scalar=-1.0, in1=prev[:], op0=ALU.mult,
                                       op1=ALU.mult).then_inc(ops_ready.sem, 1)
                need(ops_ready)
                link(v.tensor_copy(tt[:], ident[:].unsqueeze(1).broadcast_to((P, NH, P))))
                for i, pair in enumerate(MT_PAIRS):
                    need(mt_done, i)
                    hs = slice(pair[0], pair[1] + 1, 2)
                    m_ps = ps[:, mt_bank(pair[0])].rearrange("p (h x t) -> p h x t", h=2, x=4)
                    for c in range(2):
                        r = other[c]
                        v.tensor_tensor(mab[r, hs, r], m_ps[r, :, 1 + c],
                                        causal_chunk[r, 1:2].broadcast_to((HD, 2, HD)), ALU.mult)
                    v.tensor_tensor(mt[:, hs].rearrange("p h x t -> p h (x t)"), m_ps.rearrange("p h x t -> p h (x t)"),
                                    causal_chunk[:].rearrange("p x t -> p (x t)").unsqueeze(1).broadcast_to((P, 2, 4 * HD)),
                                    ALU.mult).then_inc(mt_ready.sem, 1)
                need(bonus_done)
                link(v.tensor_copy(small[:, 56:56 + NH], ps[:, 5, 0:NH]))
                need(mt_ready, NH // 2 - 1)
                link(v.transpose(wt[:], mab[:]))
                for lv in range(LEVELS):
                    if lv == 0:
                        src = first_half[0](wt[:]).rearrange("p h n b -> p h (n b)")
                    else:
                        need(q_done, lv - 1)
                        src = ps[:, 0].rearrange("p (h c) -> p h c", h=NH)
                    v.tensor_tensor(qb[:], src, level_mask[:, lv].unsqueeze(1).broadcast_to((P, NH, HD)),
                                    ALU.mult).then_inc(q_ready.sem, 1)
                    dst = first_half[lv](tt[:])
                    if lv == 0:
                        need(q_ready, 0)
                        add = qb[:].rearrange("p h (n b) -> p h n b", b=1)
                    else:
                        need(t_done, lv - 1)
                        add = ps[:, 1].rearrange("p (h n b) -> p h n b", h=NH, b=1 << lv)
                    hn = "p h n b -> p (h n) b"
                    v.tensor_tensor(dst.rearrange(hn), dst.rearrange(hn), add.rearrange(hn), ALU.add).then_inc(t_ready.sem, 1)
                    if lv < LEVELS - 1:
                        need(t_ready, lv)
                        v.transpose(wt[:], tt[:]).then_inc(tt_turned.sem, 1)
                for c in range(2):
                    need(s_done, c)
                    link(v.tensor_tensor(state[:], state[:], ps[:, 2].rearrange("p (j h v) -> p j h v", j=NJ, h=2), ALU.add))
                    st = state[:].rearrange("p j h v -> p (j h) v")
                    v.tensor_tensor(st, st, over(small[:, 64 + 8 * c:72 + 8 * c], (P, NH, HD)), ALU.mult).then_inc(s_ready.sem, 1)
                y_ps = [ps[own[c], 4 + c].rearrange("p (h v) -> p h v", h=NH) for c in range(2)]
                full = (P, NH, HD)
                for c in range(2):
                    need(y_done, c)
                    last = v.tensor_reduce(small[own[c], 40:40 + NH], y_ps[c], AX, ALU.add)
                link(last)
                link(v.tensor_scalar(small[:, 40:40 + NH], small[:, 40:40 + NH], 1.0 / HD, None, ALU.mult))
                for c in range(2):
                    last = v.tensor_tensor(y1[own[c]], y_ps[c], over(small[own[c], 40:40 + NH], (HD, NH, HD)), ALU.subtract)
                last.then_inc(y_mid.sem, 1)
                need(y_sq)
                link(v.tensor_reduce(small[:, 48:48 + NH], y2[:], AX, ALU.add))
                v.tensor_scalar(small[:, 48:48 + NH], small[:, 48:48 + NH], 1.0 / HD, GN_EPS, ALU.mult, ALU.add).then_inc(y_var.sem, 1)
                for c in range(2):
                    r = own[c]
                    last = v.tensor_tensor(y2[r], uv[r, c], over(small[r, 56:56 + NH], (HD, NH, HD)), ALU.mult)
                link(last)
                need(y_std)
                link(v.reciprocal(small[:, 48:48 + NH], small[:, 48:48 + NH]))
                link(v.tensor_tensor(y1[:], y1[:], over(small[:, 48:48 + NH], full), ALU.mult))
                lnw = [ln_wb[:, k].rearrange("p (h v) -> p h v", h=NH) for k in range(2)]
                link(v.tensor_tensor(y1[:], y1[:], lnw[0], ALU.mult))
                link(v.tensor_tensor(y1[:], y1[:], lnw[1], ALU.add))
                link(v.tensor_tensor(y1[:], y1[:], y2[:], ALU.add))
                need(g_ready)
                v.tensor_tensor(y1[:], y1[:], g_tok[:], ALU.mult).then_inc(y_ready.sem, 1)
                need(y_ready)

            ch.loop(25)

            def rwkv_pass(T):
                ch.begin(T)
                rwkv(T)

            passes(dve, rwkv_pass, NT)
            ch.end(NT)

            dve.wait_ge(dist_ready, 1)
            dve.wait_ge(y_a_ready.sem, NT)
            link(v.tensor_copy(dist_f[:], dist_i[:]))
            link(v.tensor_scalar(rem_i[:], dist_i[:], DILATION[2] // STRIDE - 1, None, ALU.bitwise_and))
            link(v.tensor_scalar(late_f[:], dist_f[:], 0.0, NEG, ALU.is_lt, ALU.mult))
            slope = [2.0 ** (-8.0 * (a + 1) / (HG * NG)) for a in range(HG * NG)]
            link(v.tensor_scalar(mask_f[:], dist_f[:], float(WINDOW), NEG, ALU.is_gt, ALU.mult))
            link(v.tensor_tensor(mask_f[:], mask_f[:], late_f[:], ALU.min))
            for hh in range(HG):
                last = v.scalar_tensor_tensor(out=bias_win[:, hh], in0=dist_f[:], scalar=-slope[hh],
                                              in1=mask_f[:], op0=ALU.mult, op1=ALU.add)
            link(last)
            link(v.tensor_copy(mask_f[:], rem_i[:]))
            link(v.tensor_scalar(mask_f[:], mask_f[:], 0.0, NEG, ALU.is_gt, ALU.mult))
            link(v.tensor_tensor(mask_f[:], mask_f[:], late_f[:], ALU.min))
            for gi in range(1, NG):
                mask = late_f if DILATION[gi] == STRIDE else mask_f
                for hh in range(HG):
                    last = v.scalar_tensor_tensor(out=bias_dil[:, (gi - 1) * HG + hh], in0=dist_f[:, P:2 * P],
                                                  scalar=-STRIDE * slope[gi * HG + hh], in1=mask[:, P:2 * P],
                                                  op0=ALU.mult, op1=ALU.add)
            link(last)

            dve.wait_ge(conv_loaded, 16)
            B0, C0, X0 = CONV_T, CONV_T + CJ, CONV_T + 2 * CJ
            link(v.tensor_tensor(cols(C0, CJ), cols(C0, CJ), cols(X0, CJ), ALU.mult))
            for t in range(CJ):
                tap = [params[:, C_CONV + k * CJ + t:C_CONV + k * CJ + t + 1] for k in range(3)]
                last = v.tensor_scalar(cols(X0 + t)[:, 0], proj[:, C0 + t, 0:SEQ], tap[0], None, ALU.mult)
            link(last)
            for k in range(1, 3):
                for t in range(CJ):
                    tap = params[:, C_CONV + k * CJ + t:C_CONV + k * CJ + t + 1]
                    last = v.scalar_tensor_tensor(out=cols(X0 + t)[:, 0], in0=proj[:, C0 + t, k:k + SEQ], scalar=tap,
                                                  in1=cols(X0 + t)[:, 0], op0=ALU.mult, op1=ALU.add)
                link(last)
            link(v.tensor_tensor(cols(B0, CJ), cols(B0, CJ), cols(X0, CJ), ALU.mult))

            for t in range(AJ):
                dve.wait_ge(v_turned, t + 1)
                v.tensor_copy(cols(ATT_T + 2 * AJ + t)[:, 0], ps[:, t]).then_inc(v_ready, 1)
            def keep_output(p):
                dve.wait_ge(pv_done, 2 * p + 2)
                if p == 0:
                    dve.wait_ge(sorted_ready, 8)
                gi, j = p // 2, p % 2
                if gi == 0:
                    v.tensor_copy(o_win[:, j], ps[:, 6 + p % 2]).then_inc(o_ready, 1)
                else:
                    v.tensor_copy(token_blocks(o_dil[:, gi - 1, j]), unsort(ps[:, 6 + p % 2])).then_inc(o_ready, 1)

            for u, (gi, hh) in enumerate(ATT_UNITS):
                dve.wait_ge(scores_done, u + 1)
                if u >= 2:
                    dve.wait_ge(probs_turned, u - 1)
                sb = 2 * (u % 2)
                top = top_of(gi)[:, :, hh]
                if gi == 0:
                    sc = ps[:, sb:sb + 2].rearrange("p a (b c) -> p (a b) c", c=2 * P)
                    pb = p_buf[:, u % 2].rearrange("p (n c) -> p n c", c=2 * P)
                    v.scalar_tensor_tensor(out=pb[:, 0, P:2 * P], in0=sc[:, 0, P:2 * P], scalar=HD ** -0.5,
                                           in1=bias_win[:, hh, P:2 * P], op0=ALU.mult, op1=ALU.add)
                    link(v.scalar_tensor_tensor(out=pb[:, 1:NT], in0=sc[:, 1:NT], scalar=HD ** -0.5,
                                                in1=bias_win[:, hh].unsqueeze(1).broadcast_to((P, NT - 1, 2 * P)),
                                                op0=ALU.mult, op1=ALU.add))
                    v.tensor_reduce(top[:, 0:1], pb[:, 0, P:2 * P], AX, ALU.max)
                    link(v.tensor_reduce(top[:, 1:NT], pb[:, 1:NT], AX, ALU.max))
                else:
                    pb = p_buf[:, u % 2, 0:SEQ].rearrange("p (n c) -> p n c", c=P)
                    link(v.scalar_tensor_tensor(out=pb, in0=ps[:, sb].rearrange("p (n c) -> p n c", c=P), scalar=HD ** -0.5,
                                                in1=bias_dil[:, (gi - 1) * HG + hh].unsqueeze(1).broadcast_to((P, NT, P)),
                                                op0=ALU.mult, op1=ALU.add))
                    link(v.tensor_reduce(top, pb, AX, ALU.max))
                v.tensor_scalar(less_top(u), top, -1.0, None, ALU.mult).then_inc(scores_max, 1)
                if u >= 3 and u % 2 == 1:
                    keep_output(u // 2 - 1)
            keep_output(len(ATT_UNITS) // 2 - 1)

            dve.wait_ge(stats_turned, 1)
            row4 = slice(0, HG)
            top4 = top_row[row4]
            link(v.tensor_copy(top4, ps[row4, 0]))
            for gi in range(1, NG):
                link(v.tensor_tensor(token_blocks(top4), token_blocks(top4), unsort(ps[row4, gi]), ALU.max))
            for gi in range(NG):
                f = (lambda a: a) if gi == 0 else token_blocks
                last = v.tensor_tensor(f(weights[row4, gi]), by_group(gi, ps[row4, gi]), f(top4), ALU.subtract)
            last.then_inc(mix_max, 1)
            dve.wait_ge(mix_exp, 1)
            link(v.tensor_tensor(den[row4, 0], weights[row4, 0], ps[row4, NG], ALU.mult))
            for gi in range(1, NG):
                link(v.tensor_tensor(token_blocks(den[row4, 1]), token_blocks(weights[row4, gi]), unsort(ps[row4, NG + gi]), ALU.mult))
                link(v.tensor_tensor(den[row4, 0], den[row4, 0], den[row4, 1], ALU.add))
            v.reciprocal(den[row4, 1], den[row4, 0]).then_inc(mix_den, 1)
            for j in range(2):
                dve.wait_ge(spread, 1 + j)
                term = top_row[:]
                link(v.tensor_tensor(y_c[:, j], o_win[:, j], ps[:, NG * j], ALU.mult))
                for gi in range(1, NG):
                    link(v.tensor_tensor(term, o_dil[:, gi - 1, j], ps[:, NG * j + gi], ALU.mult))
                    link(v.tensor_tensor(y_c[:, j], y_c[:, j], term, ALU.add))
                dve.wait_ge(spread, 3 + j)
                v.tensor_tensor(y_c[:, j], y_c[:, j], ps[:, 6 + j], ALU.mult).then_inc(y_c_ready, 1)
            dve.wait_ge(y_c_ready, 2)

            def y_part(t):
                return y_a[:, t] if t < NJ else cols(CONV_T + t - NJ)[:, 0] if t < 2 * NJ else y_c[:, t - 2 * NJ]

            for i, t in enumerate(PART_ORDER):
                dve.wait_ge(y_hi_ready, i + 1)
                v.tensor_tensor(y_lo[:, t], y_part(t), y_hi[:, t].bitcast(F), ALU.subtract).then_inc(y_lo_ready, 1)
            dve.wait_ge(g_att_ready, 1)
            for k in range(KT):
                if k < KT - 1:
                    dve.wait_ge(att_tile_done, k + 1)
                else:
                    dve.wait_ge(slot_used, S_ATT + 1)
                v.tensor_tensor(merged[:, k], ps[:, k], g_att[:, k], ALU.mult).then_inc(att_merged, 1)
            dve.wait_ge(att_merged, KT)
            for g in range(N_MERGE):
                dve.wait_ge(slot_used, S_MERGE + g + 1)
                dve.wait_ge(g_ab_ready, g + 1)
                pair = merged[:, 2 * g:2 * g + 2]
                for br in range(2):
                    b0 = 4 * (g % 2) + 2 * br
                    link(v.tensor_tensor(tmp[:], ps[:, b0:b0 + 2], g_ab[:, g % 2, br], ALU.mult))
                    last = v.tensor_tensor(pair, pair, tmp[:], ALU.add)
                    if br == 0:
                        link(last)
                last.then_inc(pair_merged, 1)
                dve.wait_ge(merged_ready, g + 1)
                v.tensor_tensor(a_lo[:, 2 * g:2 * g + 2], pair, a_hi[:, 2 * g:2 * g + 2].bitcast(F), ALU.subtract).then_inc(a_lo_ready, 1)

            dve.wait_ge(gains_loaded, 16)
            dve.wait_ge(xin_loaded, 16)
            normed(1, C_FPRE, h2_f32, KT, lambda i: add_normed(i, 0, x_in, gain_mix, x1, x1_ready) if i < NT else None)

            def ffn_in(i):
                for b in range(2):
                    n = i * 2 + b
                    bank = (S_FIN + b) % 2 * 2
                    dve.wait_ge(silu_sig, n + 1)
                    link(v.tensor_tensor(f_act[:], f_sig[:], ps[:, bank], ALU.mult))
                    v.tensor_tensor(f_act[:], f_act[:], ps[:, bank + 1], ALU.mult).then_inc(f_act_ready, 1)
                    dve.wait_ge(f_hi_ready, n + 1)
                    lo_ = f_lo[:].rearrange("p (n two) t -> p n two t", two=2)
                    hi_ = f_hi[:].rearrange("p (n two) t -> p n two t", two=2)
                    v.tensor_tensor(lo_[:, i, b], f_act[:], hi_[:, i, b].bitcast(F), ALU.subtract).then_inc(f_lo_ready, 1)
                    dve.wait_ge(f_lo_ready, n + 1)

            dve.wait_ge(a_lo_ready, NT + N_MERGE + NT)
            ch.loop(2)
            with dve.Fori(0, N_FIN // 2, 1) as i:
                ch.begin(i)
                ffn_in(i)
            ch.end(N_FIN // 2)
            dve.wait_ge(gain_ffn_loaded, 16)
            for t in range(NT):
                add_normed(t, 1, x1, gain_ffn, x1, row_ready)

        @block.tensor
        def _(pe):
            t_ = nc.tensor

            def three(dst, w0, w1, a0, a1, first, last):
                t_.matmul(dst, w0, a0, start=first, stop=False)
                t_.matmul(dst, w0, a1, start=False, stop=False)
                return t_.matmul(dst, w1, a0, start=False, stop=last)

            def by_channel(b, bank, ahi, alo, col_tiles=2):
                wh = w_hi[:, b].rearrange("p (k c) -> p k c", k=KT)
                wl = w_lo[:, b].rearrange("p (k c) -> p k c", k=KT)
                for m in range(col_tiles):
                    c = slice(m * P, (m + 1) * P)
                    for k in range(KT):
                        last = three(ps[:, bank + m], wh[:, k, c], wl[:, k, c], ahi[:, k], alo[:, k], k == 0, k == KT - 1)
                return last

            def by_token(b, ahi, alo, first, final, order=range(NT), before=lambda t: None, last_tile=NT - 1):
                wh = w_hi[:, b].rearrange("p (k c) -> p k c", k=2)
                wl = w_lo[:, b].rearrange("p (k c) -> p k c", k=2)
                for t in order:
                    before(t)
                    s_ = slice(t * P, (t + 1) * P)
                    for k in range(2):
                        for half in range(2):
                            c = slice(half * SEQ, (half + 1) * SEQ)
                            last = three(ps[:, 2 * t + half], ahi(k)[:, s_], alo(k)[:, s_], wh[:, k, c], wl[:, k, c],
                                         first and k == 0, final and k == 1)
                    if final and t < last_tile:
                        last.then_inc(z_tile_done, 1)
                return last

            pe.wait_ge(ident_ready, 1)
            pe.wait_ge(rows_loaded, 16 * 9)
            t_.transpose(ps[:, 7, 0:N_ROWS], param_rows[0:N_ROWS, :], ident[0:N_ROWS, 0:N_ROWS]).then_inc(rows_turned, 1)

            def turn_rows(src, turn):
                for t in range(NT):
                    pe.wait_ge(h_ready, turn * NT + t + 1)
                    for k in range(KT):
                        last = t_.transpose(ps[:, 2 * t + k // 4, k % 4 * P:(k % 4 + 1) * P], src[:, t, k * P:(k + 1) * P], ident[:])
                    last.then_inc(turned, 1)

            pe.wait_ge(params_ready, 1)
            turn_rows(x_tok, 0)
            pe.wait_ge(scaled, NT)
            pe.wait_ge(a_lo_ready, NT)

            def proj_pair(i):
                for b in range(2):
                    n = i * 2 + b
                    pe.wait_ge(lo_ready, n + 1)
                    if not isinstance(i, int):
                        pe.wait_ge(proj_out, n - 1)
                    by_channel(b, 2 * b, a_hi, a_lo).then_inc(slot_used, 1)

            passes(pe, proj_pair, N_RWKV // 2)
            n = N_RWKV - 1
            pe.wait_ge(lo_ready, n + 1)
            pe.wait_ge(proj_out, n - 1)
            by_channel(n % 2, 2 * (n % 2), a_hi, a_lo).then_inc(slot_used, 1)

            pe.wait_ge(consts_ready, 1)
            pe.wait_ge(ups_loaded, 48)

            def rwkv(T):
                def need(sig_, k=0):
                    pe.wait_ge(sig_.sem, sig_.at(T, k))

                def heads(t, h):
                    r = slice(HD * (h % 2), HD * (h % 2) + HD)
                    return t[r, h // 2]

                steps = iter(range(2 * PER_T * KT * 3))

                def fill_steps(count):
                    for _ in range(count):
                        u, step = divmod(next(steps), 3)
                        q, kt = u // KT, u % KT
                        k, half = q // 2, q % 2
                        b = (N_RWKV + k) % 2
                        if u % (2 * KT) == 0 and step == 0:
                            pe.wait_ge(lo_ready, T * PER_T + (N_RWKV + k + 1))
                        if kt == 0 and step == 0 and not (isinstance(T, int) and q < 2):
                            pe.wait_ge(spill_copied, T * (2 * PER_T) + (q - 1))
                        w = (w_lo if step == 2 else w_hi)[:, b].rearrange("p (k c) -> p k c", k=KT)
                        a = (a_lo if step == 1 else a_hi)[:, kt]
                        last = t_.matmul(ps[:, 6 + half], w[:, kt, half * P:(half + 1) * P], a,
                                         start=(kt == 0 and step == 0), stop=(kt == KT - 1 and step == 2))
                        if kt == KT - 1 and step == 2:
                            last.then_inc(slot_used if half else first_tile, 1)

                def fill(count):
                    fill_steps(3 * count)

                fill(12)
                need(lora_ready)
                for j in range(NJ):
                    c = slice(j * P, (j + 1) * P)
                    t_.matmul(ps[:, 0, c], lora_up[0:HD, c], xm[0:HD, RT - 2], start=True, stop=True)
                for j in range(NJ):
                    c = slice(j * P, (j + 1) * P)
                    last = t_.matmul(ps[:, 1, c], lora_up[HD:P, c], xm[HD:P, RT - 2], start=True, stop=True)
                last.then_inc(z_done.sem, 1)
                t_.matmul(ps[:, 2], xm[:, RT - 1], g_up[:], start=True, stop=True).then_inc(g_done.sem, 1)
                fill(2)
                need(sq_ready)
                t_.matmul(ps[:, 3], head_ones[:], sq[:].rearrange("p j t -> p (j t)"), start=True, stop=True).then_inc(ssq_done.sem, 1)
                fill(29)
                need(ops_ready)
                for dst, src in ((4, bkd[:, :, 0:P]), (5, bkd[:, :, P:2 * P]), (0, xm[:, 2 * NJ:3 * NJ])):
                    for j in range(NJ):
                        last = t_.transpose(ps[:, dst, j * P:(j + 1) * P], src[:, j], ident[:])
                last.then_inc(toks_done.sem, 1)
                for h in range(NH):
                    if h == 1:
                        need(g_ready)
                    if h == 5:
                        need(mt_ready, 0)
                    for c in range(2):
                        col = h // 2 % 2 * 2 * P + c * P
                        last = t_.matmul(ps[:, mt_bank(h), col:col + P], heads(bkd, h)[:, c * P:(c + 1) * P],
                                         heads(ar, h)[:, c * P:(c + 1) * P], start=True, stop=True)
                    if h // 2 % 2:
                        last.then_inc(mt_done.sem, 1)
                fill(4)
                need(toks_ready)
                for j in range(NJ):
                    last = t_.matmul(ps[:, 5, 2 * j:2 * j + 2], rk[:, j], head_ones[:, ::HD], start=True, stop=True)
                last.then_inc(bonus_done.sem, 1)
                need(mt_ready, NH // 2 - 1)
                fill(5)
                for lv in range(1, LEVELS):
                    need(t_ready, lv - 1)
                    for h in range(NH):
                        rhs = tt[:, h].rearrange("p (n two b) -> p n two b", two=2, b=1 << lv)[:, :, 0]
                        last = t_.matmul(ps[:, 0, h * HD:(h + 1) * HD].rearrange("p (n b) -> p n b", b=1 << lv), mab[:, h], rhs,
                                         start=True, stop=True)
                    last.then_inc(q_done.sem, 1)
                    fill_steps(4)
                    need(q_ready, lv)
                    need(tt_turned, lv - 1)
                    for h in range(NH):
                        last = t_.matmul(ps[:, 1, h * HD:(h + 1) * HD], wt[:, h], qb[:, h], start=True, stop=True)
                    last.then_inc(t_done.sem, 1)
                    fill_steps(5)
                need(t_ready, LEVELS - 1)
                for h in range(NH):
                    last = t_.transpose(ps[:, 3 + h // 4, h % 4 * P:(h % 4 + 1) * P], tt[:, h], ident[:])
                last.then_inc(w_done.sem, 1)
                fill(2)
                need(w_ready)
                for c in range(2):
                    r, ru = own[c], other[c]
                    if c > 0:
                        need(s_ready, c - 1)
                    elif not isinstance(T, int):
                        pe.wait_ge(s_ready.sem, T * 2)

                    for j in range(NJ):
                        t_.matmul(ps[:, 4 + c, j * P:(j + 1) * P], ar[:, j, c * P:(c + 1) * P],
                                  state[:, j].rearrange("p h v -> p (h v)"), start=(j == 0), stop=False, skip_group_check=True)
                    for h in range(NH):
                        last = t_.matmul(ps[ru, 4 + c, h * HD:(h + 1) * HD], mt[r, h, 1 + c], uv[r, c, h], start=False, stop=True,
                                         skip_group_check=True)
                    last.then_inc(x_done.sem, 1)
                    fill_steps(4)
                    need(x_ready, c)
                    fill_steps(1)
                    for h in range(NH):
                        last = t_.matmul(ps[ru, 1, h * HD:(h + 1) * HD], wt[ru, h, ru], xs[ru, h], start=True, stop=True)
                    last.then_inc(u_done.sem, 1)
                    fill_steps(4)
                    need(u_ready, c)
                    for j in range(NJ):
                        last = t_.matmul(ps[:, 2, j * P:(j + 1) * P], bk_tok[:, c, j],
                                         uv[:, c, 2 * j:2 * j + 2].rearrange("p h v -> p (h v)"), start=True, stop=True)
                    last.then_inc(s_done.sem, 1)
                    for h in range(NH):
                        last = t_.matmul(ps[r, 4 + c, h * HD:(h + 1) * HD], mt[:, h, 3 * c], uv[:, c, h], start=False, stop=True,
                                         skip_group_check=True)
                    last.then_inc(y_done.sem, 1)
                    fill_steps(5)
                fill_steps(53)
                need(y_ready)
                for j in range(NJ):
                    last = t_.transpose(ps[:, 0, j * P:(j + 1) * P], y1[:, 2 * j:2 * j + 2].rearrange("p h v -> p (h v)"), ident[:])
                last.then_inc(y_turned.sem, 1)

            passes(pe, rwkv, NT)


            def left(m, bank):
                pe.wait_ge(lo_ready, S_REST + m + 1)
                by_channel((S_REST + m) % 2, bank, a_hi, a_lo).then_inc(slot_used, 1)

            for m in range(N_LEFT - 1):
                if m == 1:
                    pe.wait_ge(y_a_ready.sem, NT)
                left(m, 2 * ((m + 1) % 2))

            pe.wait_ge(qkv_loaded, 16)
            pe.wait_ge(spill_copied, 2 * (N_WIN - N_RWKV - 1))
            for t in range(AJ):
                vt = cols(ATT_T + 2 * AJ + t)[:, 0]
                for blk in range(NT):
                    src = vt[:, blk * P:(blk + 1) * P] if t < 2 else sort_tokens(vt)[:, blk]
                    last = t_.transpose(ps[:, t, blk * P:(blk + 1) * P], src, ident[:])
                last.then_inc(v_turned, 1)
            pe.wait_ge(v_ready, AJ)

            def scores(u):
                gi, hh = ATT_UNITS[u]
                q, k = q_row(gi, hh, 0), q_row(gi, hh, 1)
                if gi == 1 and hh == 0:
                    pe.wait_ge(sorted_ready, 8)
                for n in range(NT):
                    if gi == 0:
                        k0 = max(0, n - 1)
                        dst = ps[:, 2 * (u % 2) + n // 2, (n % 2) * 2 * P + (P if n == 0 else 0):(n % 2 + 1) * 2 * P]
                    else:
                        k0 = n
                        dst = ps[:, 2 * (u % 2), n * P:(n + 1) * P]
                    last = t_.matmul(dst, q[:, n * P:(n + 1) * P], k[:, k0 * P:(n + 1) * P], start=True, stop=True)
                last.then_inc(scores_done, 1)

            def outputs(u):
                gi, hh = ATT_UNITS[u]
                pe.wait_ge(probs_t_ready, u + 1)
                if u >= 4:
                    pe.wait_ge(o_ready, u // 2 - 1)
                rows = slice(HD * (hh % 2), HD * (hh % 2) + HD)
                bl = blocks(gi)
                for i, (n, k) in enumerate(bl):
                    vt = cols(ATT_T + 2 * AJ + 2 * gi + hh // 2)[:, 0, k * P + HD * (hh % 2):k * P + HD * (hh % 2) + HD]
                    last = t_.matmul(ps[rows, 6 + u // 2 % 2, n * P:(n + 1) * P], vt, pt_buf[:, u % 2, i * P:(i + 1) * P],
                                     start=(i == 0 or bl[i - 1][0] != n), stop=(k == n))
                last.then_inc(pv_done, 1)

            scores(0)
            scores(1)
            for u, (gi, hh) in enumerate(ATT_UNITS):
                pe.wait_ge(probs_ready, u + 1)
                if u >= 1 and (gi == 0 or ATT_UNITS[u - 1][0] == 0):
                    pe.wait_ge(probs_t_ready, u)
                elif u >= 2:
                    pe.wait_ge(probs_t_ready, u - 1)
                for i, (n, k) in enumerate(blocks(gi)):
                    c = slice(P * (n + k + 1), P * (n + k + 2)) if gi == 0 else slice(P * n, P * (n + 1))
                    bank = 4 + (i // 4 if gi == 0 else u % 2)
                    last = t_.transpose(ps[:, bank, i % 4 * P:(i % 4 + 1) * P], p_buf[:, u % 2, c], ident[:])
                last.then_inc(probs_turned, 1)
                if u + 2 < len(ATT_UNITS):
                    scores(u + 2)
                if u >= 1:
                    outputs(u - 1)
            outputs(len(ATT_UNITS) - 1)
            for gi in range(NG):
                for t in range(NT):
                    t_.transpose(ps[0:HG, gi, t * P:(t + 1) * P], top_of(gi, t), ident[:])
                    last = t_.transpose(ps[0:HG, NG + gi, t * P:(t + 1) * P], sum_of(gi, t), ident[:])
            last.then_inc(stats_turned, 1)
            pe.wait_ge(o_ready, len(ATT_UNITS) // 2)
            left(N_LEFT - 1, 6)
            def spread_rows(dst, rows, j):
                return t_.matmul(dst, head_rows[0:HG, j * P:(j + 1) * P], rows, start=True, stop=True)

            pe.wait_ge(dist_ready, 2)
            pe.wait_ge(mix_exp, 1)
            for gi in range(NG):
                last = spread_rows(ps[:, gi], weights[0:HG, gi], 0)
            last.then_inc(spread, 1)
            pe.wait_ge(mix_den, 1)
            for gi in range(NG):
                last = spread_rows(ps[:, NG + gi], weights[0:HG, gi], 1)
            last.then_inc(spread, 1)
            pe.wait_ge(spill_copied, 2 * (N_WIN - N_RWKV))
            for j in range(2):
                spread_rows(ps[:, 6 + j], den[0:HG, 1], j).then_inc(spread, 1)

            pe.wait_ge(y_lo_ready, 2)
            pe.wait_ge(lo_ready, S_ATT + 1)
            b = S_ATT % 2
            wh = w_hi[:, b].rearrange("p (k c) -> p k c", k=2)
            wl = w_lo[:, b].rearrange("p (k c) -> p k c", k=2)
            for m in range(KT):
                c = slice(m * P, (m + 1) * P)
                for k in range(2):
                    last = three(ps[:, m], wh[:, k, c], wl[:, k, c], y_hi[:, 2 * NJ + k], y_lo[:, 2 * NJ + k], k == 0, k == 1)
                last.then_inc(att_tile_done if m < KT - 1 else slot_used, 1)
            pe.wait_ge(y_lo_ready, BT)
            for g in range(N_MERGE):
                b = (S_MERGE + g) % 2
                wh = w_hi[:, b].rearrange("p (k c) -> p k c", k=KT)
                wl = w_lo[:, b].rearrange("p (k c) -> p k c", k=KT)
                pe.wait_ge(lo_ready, S_MERGE + g + 1)
                if g >= 2:
                    pe.wait_ge(pair_merged, g - 1)
                else:
                    pe.wait_ge(att_merged, 4 * (g + 1))
                for br in range(2):
                    for m in range(2):
                        c = slice(m * P, (m + 1) * P)
                        for k in range(NJ):
                            kt = br * NJ + k
                            last = three(ps[:, 4 * (g % 2) + 2 * br + m], wh[:, kt, c], wl[:, kt, c], y_hi[:, kt], y_lo[:, kt],
                                         k == 0, k == NJ - 1)
                last.then_inc(slot_used, 1)

            pe.wait_ge(pair_merged, N_MERGE - 1)
            def out_slot(m, order=range(NT), before=lambda t: None):
                return by_token((S_OUT + m) % 2, lambda k: a_hi[:, 2 * m + k], lambda k: a_lo[:, 2 * m + k],
                                m == 0, m == N_OUT - 1, order, before)

            for m in range(N_OUT - 2):
                pe.wait_ge(a_lo_ready, NT + m + 1)
                pe.wait_ge(lo_ready, S_OUT + m + 1)
                out_slot(m, before=lambda t: pe.wait_ge(pair_merged, N_MERGE) if m == 0 and t == 2 else None).then_inc(slot_used, 1)
            m = N_OUT - 1
            pe.wait_ge(a_lo_ready, NT + m)
            pe.wait_ge(lo_ready, S_OUT + m)
            out_slot(m - 1, (0, 1))
            pe.wait_ge(a_lo_ready, NT + m + 1)
            pe.wait_ge(lo_ready, S_OUT + m + 1)
            out_slot(m, (0,))
            out_slot(m - 1, (2,))
            out_slot(m, (1,))
            out_slot(m - 1, (3,)).then_inc(slot_used, 1)
            out_slot(m, (2, 3)).then_inc(slot_used, 1)

            turn_rows(h2_tok, 1)
            pe.wait_ge(scaled, 2 * NT)
            pe.wait_ge(a_lo_ready, NT + N_MERGE + NT)

            def ffn_in(i):
                for b in range(2):
                    n = i * 2 + b
                    pe.wait_ge(lo_ready, n + S_FIN + 1)
                    if not isinstance(i, int):
                        pe.wait_ge(f_act_ready, n - 1)
                    par = (S_FIN + b) % 2
                    by_channel(par, 2 * par, a_hi, a_lo).then_inc(slot_used, 1)

            passes(pe, ffn_in, N_FIN // 2)
            pe.wait_ge(f_act_ready, N_FIN - 1)
            last_pair = (S_FOUT - 1) % 2
            for m in range(N_FOUT):
                pe.wait_ge(f_lo_ready, 2 * m + 2)
                pe.wait_ge(lo_ready, S_FOUT + m + 1)
                by_token((S_FOUT + m) % 2, lambda k: f_hi[:, 2 * m + k], lambda k: f_lo[:, 2 * m + k],
                         m == 0, m == N_FOUT - 1, *([(2, 3, 1 - last_pair, last_pair),
                                                     lambda t: pe.wait_ge(f_act_ready, N_FIN) if t == last_pair else None] if m == 0 else [])).then_inc(slot_used, 1)


_INS = ["x", "norm_mix_pre", "norm_mix_post", "norm_ffn_pre", "norm_ffn_post", "w_in", "rwkv_mu", "rwkv_w0", "rwkv_w_up",
        "rwkv_a0", "rwkv_a_up", "rwkv_g_up", "rwkv_k_k", "rwkv_k_a", "rwkv_r_k", "rwkv_ln_w", "rwkv_ln_b", "conv_w",
        "w_branch", "w_out", "w_ffn_in", "w_ffn_out"]


def kernel(**inputs):
    import numpy as _np
    import concourse.bacc as _bacc
    from concourse.bass_utils import run_bass_kernel_spmd as _run

    nc = _bacc.Bacc("TRN2", target_bir_lowering=False, num_devices=1)
    arrays, args = {}, []
    for name in _INS:
        a = _np.ascontiguousarray(inputs[name])
        arrays[name] = a
        args.append(nc.dram_tensor(name, a.shape, mybir.dt.from_np(a.dtype), kind="ExternalInput").ap())
    shape = inputs["x"].shape
    args.append(nc.dram_tensor("out", shape, mybir.dt.float32, kind="ExternalOutput").ap())
    args.append(nc.dram_tensor("spill", ((inputs["w_in"].shape[2] - inputs["rwkv_mu"].shape[1]) // 128, 128, shape[1]), mybir.dt.float32, kind="Internal").ap())
    hybrid_layer(nc, *args)
    r = _run(nc, [arrays], core_ids=[0])
    return r.results[0]["out"]
```
